# Optimizing a Trainium2 kernel written in Bass

```python
import jax, jax.numpy as jnp
from jax import lax
import numpy as np

D_MODEL = 1024
BATCH = 1
SEQ = 256
DEPTH = 2

CHUNK = 64
WINDOW = 128
WINDOW_CHUNKS = WINDOW // CHUNK
EPS = 1e-6
NEG_INF = -1e30

N_Q_HEADS = 8
N_KV_HEADS = 2
HEAD_DIM = 64
ATTN_WIDTH = N_Q_HEADS * HEAD_DIM
KV_WIDTH = N_KV_HEADS * HEAD_DIM

GLA_HEADS = 4
GLA_WIDTH = D_MODEL - ATTN_WIDTH
GLA_HEAD_V = GLA_WIDTH // GLA_HEADS
GLA_KEY_WIDTH = GLA_WIDTH // 2
GLA_HEAD_K = GLA_KEY_WIDTH // GLA_HEADS
GATE_RANK = 16
GATE_TAU = 16.0

D_FF = 2816

IN_COLS = ATTN_WIDTH + 2 * KV_WIDTH + 2 * GLA_KEY_WIDTH + GLA_WIDTH + GATE_RANK + GLA_WIDTH

kernel_name = "hymba_swa_sink_gla_macaron"

def rmsnorm(x, g):
    xf = x.astype(jnp.float32)
    y = xf * lax.rsqrt(jnp.mean(xf * xf, axis=-1, keepdims=True) + EPS)
    return (y * g.astype(jnp.float32)).astype(x.dtype)

def swiglu(x, w_gate, w_up, w_down):
    a = jnp.einsum('bsd,df->bsf', x, w_gate)
    u = jnp.einsum('bsd,df->bsf', x, w_up)
    return jnp.einsum('bsf,fd->bsd', jax.nn.silu(a) * u, w_down)

def alibi_slopes(n_heads):
    return jnp.exp2(-8.0 * jnp.arange(1, n_heads + 1, dtype=jnp.float32) / n_heads)

def sliding_window_attention(q, k, v, sinks):
    B, S = q.shape[0], q.shape[1]
    nc = S // CHUNK
    grp = N_Q_HEADS // N_KV_HEADS
    qc = q.reshape(B, nc, CHUNK, N_KV_HEADS, grp, HEAD_DIM)
    kc = k.reshape(B, nc, CHUNK, N_KV_HEADS, HEAD_DIM)
    vc = v.reshape(B, nc, CHUNK, N_KV_HEADS, HEAD_DIM)

    def shift(t, w):
        return jnp.pad(t, ((0, 0), (w, 0), (0, 0), (0, 0), (0, 0)))[:, :nc]

    kw = jnp.concatenate([shift(kc, w) for w in range(WINDOW_CHUNKS - 1, -1, -1)], axis=2)
    vw = jnp.concatenate([shift(vc, w) for w in range(WINDOW_CHUNKS - 1, -1, -1)], axis=2)

    scores = jnp.einsum('bnqhgd,bnkhd->bnhgqk', qc, kw,
                        preferred_element_type=jnp.float32) * (HEAD_DIM ** -0.5)
    qpos = (WINDOW_CHUNKS - 1) * CHUNK + jnp.arange(CHUNK)
    kpos = jnp.arange(WINDOW_CHUNKS * CHUNK)
    dist = jnp.abs(qpos[:, None] - kpos[None, :]).astype(jnp.float32)
    slopes = alibi_slopes(N_Q_HEADS).reshape(N_KV_HEADS, grp)
    bias = -slopes[:, :, None, None] * dist
    src_chunk = jnp.arange(nc)[:, None] - (WINDOW_CHUNKS - 1) + (kpos // CHUNK)[None, :]
    valid = (src_chunk >= 0)[None, :, None, None, None, :]
    scores = jnp.where(valid, scores + bias, NEG_INF)
    sink = jnp.broadcast_to(sinks.astype(jnp.float32).reshape(1, 1, N_KV_HEADS, grp, 1, 1),
                            scores.shape[:-1] + (1,))
    probs = jax.nn.softmax(jnp.concatenate([scores, sink], axis=-1), axis=-1)[..., :-1]
    out = jnp.einsum('bnhgqk,bnkhd->bnqhgd', probs.astype(v.dtype), vw)
    return out.reshape(B, S, N_Q_HEADS * HEAD_DIM)

def gla_chunked(q, k, v, log_a):
    B, S = q.shape[0], q.shape[1]
    nc = S // CHUNK
    f32 = jnp.float32
    q = q.astype(f32).reshape(B, nc, CHUNK, GLA_HEADS, GLA_HEAD_K) * (GLA_HEAD_K ** -0.5)
    k = k.astype(f32).reshape(B, nc, CHUNK, GLA_HEADS, GLA_HEAD_K)
    v = v.astype(f32).reshape(B, nc, CHUNK, GLA_HEADS, GLA_HEAD_V)
    la = log_a.astype(f32).reshape(B, nc, CHUNK, GLA_HEADS, GLA_HEAD_K)
    b = lax.cumsum(la, axis=2)
    b_last = b[:, :, -1]
    q_e = q * jnp.exp(b)
    k_e = k * jnp.exp(-b)
    k_end = k * jnp.exp(b_last[:, :, None] - b)
    causal = jnp.tril(jnp.ones((CHUNK, CHUNK), dtype=bool))
    attn = jnp.where(causal, jnp.einsum('bnihd,bnjhd->bnhij', q_e, k_e), 0.0)
    o_intra = jnp.einsum('bnhij,bnjhv->bnihv', attn, v)
    chunk_upd = jnp.einsum('bnjhd,bnjhv->bnhdv', k_end, v)
    chunk_decay = jnp.exp(b_last)

    def step(state, inp):
        dec, upd = inp
        return dec[..., None] * state + upd, state

    init = jnp.zeros((B, GLA_HEADS, GLA_HEAD_K, GLA_HEAD_V), f32)
    _, s_before = lax.scan(step, init, (jnp.swapaxes(chunk_decay, 0, 1), jnp.swapaxes(chunk_upd, 0, 1)))
    s_before = jnp.swapaxes(s_before, 0, 1)
    o_inter = jnp.einsum('bnihd,bnhdv->bnihv', q_e, s_before)
    return (o_intra + o_inter).reshape(B, S, GLA_HEADS, GLA_HEAD_V)

def hybrid_mixer(h, w_in, attn_sinks, attn_out_norm, gla_gate_up, gla_gate_bias, gla_out_norm, w_out):
    B, S, _ = h.shape
    proj = jnp.einsum('bsd,dc->bsc', h, w_in)
    sizes = [ATTN_WIDTH, KV_WIDTH, KV_WIDTH, GLA_KEY_WIDTH, GLA_KEY_WIDTH, GLA_WIDTH, GATE_RANK, GLA_WIDTH]
    cuts = np.cumsum(sizes)[:-1].tolist()
    q_a, k_a, v_a, q_g, k_g, v_g, gate_lr, r_g = jnp.split(proj, cuts, axis=-1)

    attn = sliding_window_attention(q_a.reshape(B, S, N_Q_HEADS, HEAD_DIM),
                                    k_a.reshape(B, S, N_KV_HEADS, HEAD_DIM),
                                    v_a.reshape(B, S, N_KV_HEADS, HEAD_DIM), attn_sinks)
    attn = rmsnorm(attn, attn_out_norm)

    gate_logit = jnp.einsum('bsr,rk->bsk', gate_lr, gla_gate_up) + gla_gate_bias
    log_a = jax.nn.log_sigmoid(gate_logit.astype(jnp.float32)) / GATE_TAU
    o = gla_chunked(q_g.reshape(B, S, GLA_HEADS, GLA_HEAD_K),
                    k_g.reshape(B, S, GLA_HEADS, GLA_HEAD_K),
                    v_g.reshape(B, S, GLA_HEADS, GLA_HEAD_V),
                    log_a.reshape(B, S, GLA_HEADS, GLA_HEAD_K))
    o = rmsnorm(o, gla_out_norm) * jax.nn.silu(r_g.astype(jnp.float32).reshape(B, S, GLA_HEADS, GLA_HEAD_V))
    gla = o.reshape(B, S, GLA_WIDTH).astype(h.dtype)

    mixed = jnp.concatenate([attn, gla], axis=-1)
    return jnp.einsum('bsc,cd->bsd', mixed, w_out)

def setup_inputs(seed: int = 0) -> dict:
    key = jax.random.key(seed)
    ks = jax.random.split(key, 24)
    nrm = lambda k, shape, scale: jax.random.normal(k, shape, jnp.float32) * scale
    gain = lambda k, shape: 1.0 + 0.02 * jax.random.normal(k, shape, jnp.float32)
    L, D, F = DEPTH, D_MODEL, D_FF
    return {
        "x": jax.random.normal(ks[0], (BATCH, SEQ, D), jnp.float32),
        "ffn1_norm": gain(ks[1], (L, D)),
        "ffn1_w_gate": nrm(ks[2], (L, D, F), D ** -0.5),
        "ffn1_w_up": nrm(ks[3], (L, D, F), D ** -0.5),
        "ffn1_w_down": nrm(ks[4], (L, F, D), F ** -0.5),
        "mix_norm": gain(ks[5], (L, D)),
        "w_in": nrm(ks[6], (L, D, IN_COLS), D ** -0.5),
        "attn_sinks": nrm(ks[7], (L, N_Q_HEADS), 0.5),
        "attn_out_norm": gain(ks[8], (L, ATTN_WIDTH)),
        "gla_gate_up": nrm(ks[9], (L, GATE_RANK, GLA_KEY_WIDTH), GATE_RANK ** -0.5),
        "gla_gate_bias": nrm(ks[10], (L, GLA_KEY_WIDTH), 0.1),
        "gla_out_norm": gain(ks[11], (L, GLA_HEAD_V)),
        "w_out": nrm(ks[12], (L, D, D), D ** -0.5),
        "ffn2_norm": gain(ks[13], (L, D)),
        "ffn2_w_gate": nrm(ks[14], (L, D, F), D ** -0.5),
        "ffn2_w_up": nrm(ks[15], (L, D, F), D ** -0.5),
        "ffn2_w_down": nrm(ks[16], (L, F, D), F ** -0.5),
        "final_norm": gain(ks[17], (D,)),
    }

def reference(x, ffn1_norm, ffn1_w_gate, ffn1_w_up, ffn1_w_down, mix_norm, w_in, attn_sinks,
              attn_out_norm, gla_gate_up, gla_gate_bias, gla_out_norm, w_out, ffn2_norm,
              ffn2_w_gate, ffn2_w_up, ffn2_w_down, final_norm):
    for l in range(DEPTH):
        x = x + 0.5 * swiglu(rmsnorm(x, ffn1_norm[l]), ffn1_w_gate[l], ffn1_w_up[l], ffn1_w_down[l])
        x = x + hybrid_mixer(rmsnorm(x, mix_norm[l]), w_in[l], attn_sinks[l], attn_out_norm[l],
                             gla_gate_up[l], gla_gate_bias[l], gla_out_norm[l], w_out[l])
        x = x + 0.5 * swiglu(rmsnorm(x, ffn2_norm[l]), ffn2_w_gate[l], ffn2_w_up[l], ffn2_w_down[l])
    return rmsnorm(x, final_norm)


_drawn_inputs = setup_inputs


def setup_inputs(seed=0):
    import zlib

    import numpy as np

    out = dict(_drawn_inputs(seed))
    spreads = {}
    factors = {'ffn1_norm': 3.634,
     'attn_out_norm': 13.384,
     'gla_gate_bias': 2.728,
     'gla_out_norm': 20.429,
     'ffn2_norm': 6.114,
     'final_norm': 8.248,
     'attn_sinks': 4.845}
    for name, (base, spread) in spreads.items():
        noise = np.random.default_rng([zlib.crc32(name.encode()), seed]).standard_normal(out[name].shape)
        drawn = base * np.exp(spread * noise) if base else spread * noise
        out[name] = __import__('jax').numpy.asarray(drawn.astype(out[name].dtype))
    for name, factor in factors.items():
        out[name] = (out[name] * factor).astype(out[name].dtype)
    return out
```

```python
from contextlib import ExitStack

import concourse.bass as bass
from concourse import mybir

F32 = mybir.dt.float32
F32R = mybir.dt.float32r
I32 = mybir.dt.int32
ALU = mybir.AluOpType
ACT = mybir.ActivationFunctionType
AX = mybir.AxisListType

P = 128
SEQ = 256
D = 1024
DEPTH = 2
KT = D // P
TT = SEQ // P
FF = 2816
UC = 256
GROUPS = FF // UC
FT = UC // P
CHUNK = 64
NCH = SEQ // CHUNK
HEADS = 8
HD = 64
GH = 4
DK = 64
RANK = 16
TAU = 16.0
EPS = 1e-6
SLOT = KT * UC

C_Q, C_K, C_V = 0, 512, 640
C_QG, C_KG, C_VG, C_LR, C_RG = 768, 1024, 1280, 1792, 1808
IN_COLS = 2320

G_MIX, G_FFN2, G_NEXT = 0, KT, 2 * KT
G_ATT = 3 * KT
G_BIAS = G_ATT + 4
G_GLA = G_BIAS + 2
G_SINK = G_GLA + 1
G_UP = G_SINK + HEADS
NPAR = G_UP + 256

K_DIST, K_MASK, K_ID = 0, 384, 512
NCST = 640

FU = 3 * GROUPS
MU = 15
LU = 2 * FU + MU
FFN_TURN = (0, (FU + MU) // 3)
MIX_TURN = FU // 3
TURNS = LU // 3
WIDTH = [KT * UC, KT * RANK] + [KT * UC] * 8 + [D, D, 2 * D, 2 * D, 2 * D]
WO_K = [(0,), (1,), (2, 3), (4, 5), (6, 7)]
(M_KV, M_LR, M_Q0, M_Q1, M_QG, M_KG, M_V0, M_V1, M_R0, M_R1) = range(10)
M_WO = 10
PAIRED = [M_Q0, M_Q1, M_WO, M_WO + 1, M_WO + 2]
M_BANK = [0, 1, 2, 0, 1, 2, 0, 1, 2, 0]

ST = 1
RS = 12
MAGIC = float(0x5F3759DF)


def head(s):
    return s // 2 + 4 * (s % 2)


def trunk(nc, xt, par_d, gain0_d, cst_d, fg, fu, fd, w_in, w_out, out):
    ctx = ExitStack()
    with ctx:
        def sb(name, shape, dt=F32):
            return ctx.enter_context(nc.sbuf_tensor(name, shape, dt))

        def sem(name):
            return ctx.enter_context(nc.semaphore(name))

        raw = sb("raw", [P, 3, SLOT])
        whi = sb("whi", [P, 3, SLOT], F32R)
        wlo = sb("wlo", [P, 3, SLOT], F32R)
        resid = sb("resid", [P, KT, SEQ])
        xhi = sb("xhi", [P, KT, SEQ], F32R)
        xlo = sb("xlo", [P, KT, SEQ], F32R)
        sq = sb("sq", [P, KT, SEQ])
        sqsum = sb("sqsum", [P, SEQ])
        sqsum_a = sb("sqsum_a", [P, SEQ])
        par = sb("par", [P, NPAR])
        gain0 = sb("gain0", [P, KT])
        cst = sb("cst", [P, NCST])
        ones = sb("ones", [P, P])
        keep = sb("keep", [P, SEQ])
        rs_v = sb("rs_v", [P, 8])
        rs_t = sb("rs_t", [P, 8], I32)
        rs_a = sb("rs_a", [P, 8])
        rs_y = sb("rs_y", [P, 8])
        rcol = sb("rcol", [P, TT])
        diag = sb("diag", [P, 8, P])
        rB = sb("rB", [P, SEQ])
        work = sb("work", [P, 4 * FT, SEQ])
        a32, s32, u32, h32 = (work[:, FT * i:FT * (i + 1), :] for i in range(4))
        hhi = [sb(f"hhi{i}", [P, FT, SEQ], F32R) for i in range(2)]
        hlo = [sb(f"hlo{i}", [P, FT, SEQ], F32R) for i in range(2)]
        kv = sb("kv", [P, 2, SEQ])
        qT = sb("qT", [P, 4, SEQ])
        glr = sb("glr", [RANK, SEQ])
        va = sb("va", [P, TT, P])
        z = sb("z", [P, 2, SEQ])
        az = sb("az", [P, 2, SEQ])
        la = sb("la", [P, 2, SEQ])
        bb = sb("bb", [P, 2, SEQ])
        bd = sb("bd", [P, 2, SEQ])
        eb = sb("eb", [P, 2, SEQ])
        enb = sb("enb", [P, 2, SEQ])
        qe = sb("qe", [P, 2, SEQ])
        kg = sb("kg", [P, 2, SEQ])
        ke = sb("ke", [P, 2, SEQ])
        kend = sb("kend", [P, 2, SEQ])
        ket = sb("ket", [P, 4, P])
        S = sb("S", [P, HEADS, 3 * P])
        PT = sb("PT", [P, HEADS, 3 * P])
        mx = sb("mx", [P, HEADS, 2])
        nm = sb("nm", [P, HEADS, 2])
        ds = sb("ds", [P, HEADS, 2])
        es = sb("es", [P, HEADS, 2])
        L = sb("L", [P, HEADS, 2])
        Lt = sb("Lt", [P, HEADS, 2])
        Li = sb("Li", [P, HEADS, 2])
        vg = sb("vg", [P, TT, 4 * P])
        AT = sb("AT", [P, 8, P])
        Sta = sb("Sta", [P, 3, 2, P])
        sg = sb("sg", [P, 4, SEQ])
        at32 = work[:, 0:4, :]
        o32 = work[:, 4:8, :]

        ps = [ctx.enter_context(nc.psum_tensor(f"ps{i}", [P, 512], F32)) for i in range(8)]
        acc = [ps[4 + i][:, :].rearrange("p (m t) -> p m t", m=2) for i in range(4)]

        def tiles(bank):
            return ps[bank][:, :].rearrange("p (m t) -> p m t", m=2)

        def split_views(slot, width, halves):
            r, h, lo = raw[:, slot, 0:width], whi[:, slot, 0:width], wlo[:, slot, 0:width]
            if halves:
                r = r.rearrange("p (h n c) -> p h n c", h=2, c=HD)
                h, lo = (w.rearrange("p (n h c) -> p h n c", h=2, c=HD) for w in (h, lo))
            return r, h, lo

        ident = cst[:, K_ID:K_ID + P]
        dist = cst[:, K_DIST:K_DIST + 384]
        mask = cst[:, K_MASK:K_MASK + P].bitcast(I32)

        loaded = [sem(f"loaded{i}") for i in range(3)]
        waits_met = sem("waits_met")
        half_loaded = sem("half_loaded")
        s_x = [sem(f"x_loaded{p}") for p in range(KT // 2)]
        s_gain0 = sem("gain0_loaded")
        s_par = sem("par_loaded")
        s_cst = sem("cst_loaded")
        s_set = sem("buffers_set")
        s_keep = sem("keep_set")
        rcol_done = sem("rcol_done")
        hi_done = sem("hi_done")
        lo_done = sem("lo_done")
        unit_done = sem("unit_done")
        acc_pair = sem("acc_pair")
        resid_up = sem("resid_up")
        xhi_done = sem("xhi_done")
        xlo_done = sem("xlo_done")
        sq_done = sem("sq_done")
        pool_step = sem("pool_step")
        sqsum_done = sem("sqsum_done")
        ss_done = sem("ss_done")
        rs_step = sem("rs_step")
        diag_done = sem("diag_done")
        rb_ps = sem("rb_ps")
        rb_done = sem("rb_done")
        a_done, silu_done, u_done, h_done, hhi_done, hlo_done = (
            sem(n) for n in ("a_done", "silu_done", "u_done", "h_done", "hhi_done", "hlo_done"))
        kv_ev, lr_ev, q_ev = sem("kv_ev"), sem("lr_ev"), sem("q_ev")
        vt_ps, va_ev, logit_ps = sem("vt_ps"), sem("va_ev"), sem("logit_ps")
        z_ev, gate_act, lg_done, la_done, b_done, bd_done = (
            sem(n) for n in ("z_ev", "gate_act", "lg_done", "la_done", "b_done", "bd_done"))
        eb_done, enb_done, eend_done = sem("eb_done"), sem("enb_done"), sem("eend_done")
        qg_ev, qe_done, kg_ev, ke_done, kend_done = (
            sem(n) for n in ("qg_ev", "qe_done", "kg_ev", "ke_done", "kend_done"))
        sc_ps, S_ev, max_done, soft_step, nm_done, ds_done = (
            sem(n) for n in ("sc_ps", "S_ev", "max_done", "soft_step", "nm_done", "ds_done"))
        exp_done, es_done, inv_step, pn_done = (
            sem(n) for n in ("exp_done", "es_done", "inv_step", "pn_done"))
        ket_ps, ket_ev, pt_ps, pt_ev, pv_ps, at_ev = (
            sem(n) for n in ("ket_ps", "ket_ev", "pt_ps", "pt_ev", "pv_ps", "at_ev"))
        v_ev, A_ps, A_ev, upd_ps, st_done = (sem(n) for n in ("v_ev", "A_ps", "A_ev", "upd_ps", "st_done"))
        rg_ev, sg_done, o_ps, o_ev, og_done = (sem(n) for n in ("rg_ev", "sg_done", "o_ps", "o_ev", "og_done"))
        asq_done, asum_done, ass_done, adiag_done, rA_ps = (
            sem(n) for n in ("asq_done", "asum_done", "ass_done", "adiag_done", "rA_ps"))
        osq_done, oss_done, odiag_done, rG_ps = (
            sem(n) for n in ("osq_done", "oss_done", "odiag_done", "rG_ps"))
        am_done, mhi_done, mlo_done = sem("am_done"), sem("mhi_done"), sem("mlo_done")
        s_fin, s_out = sem("fin"), sem("stored")

        block = ctx.enter_context(nc.Block())

        @block.sync
        def _(sp):
            def load(slot, turn, src, width, shape, first=False):
                if not first:
                    sp.wait_ge(lo_done, 3 * turn + slot - 2)
                    sp.sem_inc(waits_met, 1)
                dst = raw[:, slot, 0:width]
                if shape:
                    dst = dst.rearrange(*shape[0], **shape[1])
                sp.dma_start(dst, src).then_inc(loaded[slot], 16)

            by_k = (("p (k c) -> p k c",), dict(k=KT))
            by_f = (("p (k c) -> p k c",), dict(k=FT))

            def up_unit(w, l, g):
                return w[bass.ds(l, 1), :, bass.ds(g * UC, UC)].rearrange("a (k p) c -> p (a k) c", p=P)

            def down_unit(w, l, g):
                return w[bass.ds(l, 1), bass.ds(g * UC, UC), :].rearrange("a (k p) c -> p (a k) c", p=P)

            def group0(f, l, turn, first=False):
                load(0, turn, up_unit(fg[f], l, 0), SLOT, by_k, first)
                load(1, turn, up_unit(fu[f], l, 0), SLOT, by_k, first)

            def group(f, l, g, turn):
                load(2, turn + g - 1, up_unit(fg[f], l, g), SLOT, by_k)
                load(0, turn + g, up_unit(fu[f], l, g), SLOT, by_k)
                load(1, turn + g, down_unit(fd[f], l, g - 1), SLOT, by_f)

            for m in range(0, KT, 2):
                sp.dma_start(resid[:, m:m + 2, :], xt[:, m:m + 2, :]).then_inc(s_x[m // 2], 16)
                if m == 0:
                    sp.dma_start(gain0[:, :], gain0_d).then_inc(s_gain0, 16)
            group0(0, 0, 0, first=True)
            sp.dma_start(cst[:, :], cst_d).then_inc(s_cst, 16)
            load(2, 0, up_unit(fg[0], 0, 1), SLOT, by_k, first=True)

            with sp.Fori(0, DEPTH) as l:
                t0 = l * TURNS
                load(0, t0 + 1, up_unit(fu[0], l, 1), SLOT, by_k)
                load(1, t0 + 1, down_unit(fd[0], l, 0), SLOT, by_f)
                sp.wait_ge(xlo_done, KT * (3 * l + 1))
                sp.sem_inc(waits_met, 1)
                sp.dma_start(par[:, :], par_d[bass.ds(l, 1), :, :].rearrange("a p n -> p (a n)")).then_inc(s_par, 16)
                with sp.Fori(2, GROUPS) as g:
                    group(0, l, g, t0)
                load(2, t0 + GROUPS - 1, down_unit(fd[0], l, GROUPS - 1), SLOT, by_f)

                tm = t0 + MIX_TURN
                wi = w_in[bass.ds(l, 1), :, :].rearrange("a (k p) c -> p (a k) c", p=P)
                cols = {M_KV: C_K, M_LR: C_LR, M_QG: C_QG, M_KG: C_KG, M_V0: C_VG, M_V1: C_VG + UC,
                        M_R0: C_RG, M_R1: C_RG + UC}
                for i in range(MU):
                    if i in cols:
                        n = WIDTH[i] // KT
                        src, shape = wi[:, :, cols[i]:cols[i] + n], by_k
                    elif i in PAIRED:
                        if i in (M_Q0, M_Q1):
                            c = C_Q + (i - M_Q0) * P
                            dst = raw[:, i % 3, :].rearrange("p (h k c) -> p h k c", h=2, k=KT)
                            halves = [(dst[:, h], wi[:, :, c + h * 4 * HD:c + h * 4 * HD + P]) for h in range(2)]
                        else:
                            ks = WO_K[i - M_WO]
                            wo = w_out[bass.ds(l, 1), 0:512, :].rearrange("a (h j p) c -> h p (a j) c", h=2, p=HD)
                            halves = [(raw[HD * h:HD * h + HD, i % 3, 0:WIDTH[i]].rearrange(
                                "p (k c) -> p k c", k=len(ks)), wo[h, :, ks[0]:ks[-1] + 1, :]) for h in range(2)]
                        sp.wait_ge(lo_done, 3 * (tm + i // 3) + i % 3 - 2)
                        sp.sem_inc(waits_met, 1)
                        sp.dma_start(*halves[0]).then_inc(half_loaded, 16)
                        sp.dma_start(*halves[1]).then_inc(loaded[i % 3], 16)
                        continue
                    else:
                        ks = WO_K[i - M_WO]
                        shape = (("p (k c) -> p k c",), dict(k=len(ks)))
                        src = w_out[bass.ds(l, 1), ks[0] * P:(ks[-1] + 1) * P, :].rearrange(
                            "a (k p) c -> p (a k) c", p=P)
                    load(i % 3, tm + i // 3, src, WIDTH[i], shape)

                t1 = t0 + FFN_TURN[1]
                group0(1, l, t1)
                with sp.Fori(1, GROUPS) as g:
                    group(1, l, g, t1)
                load(2, t1 + GROUPS - 1, down_unit(fd[1], l, GROUPS - 1), SLOT, by_f)
                with sp.If(l < DEPTH - 1):
                    nxt = nc.s_assert_within(l + 1, 1, DEPTH - 1,
                                             skip_runtime_bounds_check_because="the branch is taken for l < DEPTH - 1")
                    group0(0, nxt, t0 + TURNS)
                    load(2, t0 + TURNS, up_unit(fg[0], nxt, 1), SLOT, by_k)
            for m in range(KT // 2):
                sp.wait_ge(s_fin, m + 1)
                sp.dma_start(out[:, 2 * m:2 * m + 2, :], sq[:, 2 * m:2 * m + 2, :]).then_inc(s_out, 16)
            sp.wait_ge(s_out, 16 * (KT // 2))

        @block.tensor
        def _(pe):
            def three(o, w_hi, w_lo, x_hi, x_lo, start, stop):
                pe.matmul(o, w_hi, x_hi, start=start, stop=False, skip_group_check=True)
                pe.matmul(o, w_hi, x_lo, start=False, stop=False, skip_group_check=True)
                return pe.matmul(o, w_lo, x_hi, start=False, stop=stop, skip_group_check=True)

            def split_ready(slot, turn):
                pe.wait_ge(lo_done, 3 * turn + slot + 1)

            def weights(slot, k, per, a, n):
                return (whi[:, slot, k * per + a:k * per + a + n], wlo[:, slot, k * per + a:k * per + a + n])

            def up_tile(o, slot, ft, v=None, ks=range(KT)):
                for k in ks:
                    if v is not None:
                        pe.wait_ge(xlo_done, KT * v + k + 1)
                    w_hi, w_lo = weights(slot, k, UC, ft * P, P)
                    last = three(o, w_hi, w_lo, xhi[:, k, :], xlo[:, k, :], k == 0, k == KT - 1)
                return last

            def up(slot, turn, bank, v=None):
                split_ready(slot, turn)
                for ft in range(FT):
                    last = up_tile(tiles(bank)[:, ft, :], slot, ft, v if ft == 0 else None)
                last.then_inc(unit_done, 1)

            def down(slot, turn, hb, first):
                split_ready(slot, turn)
                for ft in range(FT):
                    for m in range(KT):
                        w_hi, w_lo = weights(slot, ft, D, m * P, P)
                        last = three(acc[m // 2][:, m % 2, :], w_hi, w_lo, hhi[hb][:, ft, :], hlo[hb][:, ft, :],
                                     first and ft == 0 and m % 2 == 0, False)
                last.then_inc(unit_done, 1)

            def finish(slot, turn, per_k, x_hi, x_lo, pairs):
                split_ready(slot, turn)
                for m in range(KT):
                    for n, (h, lo) in enumerate(zip(x_hi, x_lo)):
                        w_hi, w_lo = weights(slot, n, per_k, m * P, P)
                        last = three(acc[m // 2][:, m % 2, :], w_hi, w_lo, h, lo, False, n == len(x_hi) - 1)
                    if m == KT - 1:
                        last.then_inc(unit_done, 1)
                    elif m % 2:
                        last.then_inc(acc_pair, 1)

            def square_sums(v):
                pe.wait_ge(sqsum_done, v + 1)
                for t in range(TT):
                    last = pe.matmul(ps[3][:, t:t + 1], sqsum[:, t * P:(t + 1) * P], ones[:, 0:1],
                                     start=True, stop=True, skip_group_check=True)
                last.then_inc(ss_done, 1)

            def spread_r(v):
                pe.wait_ge(diag_done, v + 1)
                pe.matmul(ps[3][:, 256:512], ones[:, :], diag[:, 0:2, :].rearrange("p a b -> p (a b)"),
                          start=True, stop=True, skip_group_check=True).then_inc(rb_ps, 1)

            def ffn(f, l):
                t = l * TURNS + FFN_TURN[f]
                v = 3 * l + 2 * f
                grp = (2 * l + f) * GROUPS
                split_ready(0, t)
                up_tile(tiles(0)[:, 0, :], 0, 0, v)
                up_tile(tiles(0)[:, 1, :], 0, 1, None, range(0, 3))
                square_sums(v)
                up_tile(tiles(0)[:, 1, :], 0, 1, None, range(3, KT)).then_inc(unit_done, 1)
                split_ready(1, t)
                up_tile(tiles(1)[:, 0, :], 1, 0)
                spread_r(v)
                up_tile(tiles(1)[:, 1, :], 1, 1).then_inc(unit_done, 1)
                pe.wait_ge(a_done, grp + 1)
                up(2, t, 0)
                pe.wait_ge(u_done, grp + 1)
                up(0, t + 1, 1)
                pe.wait_ge(hlo_done, grp + 1)
                if f:
                    pe.wait_ge(resid_up, 4 * (3 * l + 3))
                else:
                    pe.wait_ge(resid_up, 4 * (3 * l + 1))
                down(1, t + 1, 0, True)
                with pe.Fori(2, GROUPS) as g:
                    pe.wait_ge(a_done, grp + g)
                    up(2, t + g - 1, 0)
                    pe.wait_ge(u_done, grp + g)
                    up(0, t + g, 1)
                    pe.wait_ge(hlo_done, grp + g)
                    down(1, t + g, 0, False)
                pe.wait_ge(hlo_done, grp + GROUPS)
                finish(2, t + GROUPS - 1, D, [hhi[1][:, i, :] for i in range(FT)],
                       [hlo[1][:, i, :] for i in range(FT)], True)

            def project(i, t, o, cols=None, m=P):
                slot, turn = i % 3, t + i // 3
                split_ready(slot, turn)
                per = WIDTH[i] // KT
                for ft in range(max(1, per // P)):
                    for k in range(KT):
                        w_hi, w_lo = weights(slot, k, per, ft * P, m)
                        last = three(o[:, ft, :], w_hi, w_lo, xhi[:, k, :], xlo[:, k, :], k == 0, k == KT - 1)
                last.then_inc(unit_done, 1)

            def project_tokens(i, t, o):
                slot, turn = i % 3, t + i // 3
                split_ready(slot, turn)
                for tt in range(TT):
                    for k in range(KT):
                        w_hi, w_lo = weights(slot, k, UC, 0, UC)
                        x = slice(tt * P, (tt + 1) * P)
                        last = three(o[:, tt, :], xhi[:, k, x], xlo[:, k, x], w_hi, w_lo, k == 0, k == KT - 1)
                last.then_inc(unit_done, 1)

            def scores(s, l):
                j, b, bank = s // 2, HD * (s % 2), 5 + s % 3
                if s == 0:
                    pe.wait_ge(resid_up, 4 * (3 * l + 2))
                if s >= 3:
                    pe.wait_ge(S_ev, HEADS * l + s - 2)
                for t, (a, n) in enumerate(((0, P), (P, SEQ))):
                    last = pe.matmul(ps[bank][:, a:a + n], qT[b:b + HD, j, t * P:(t + 1) * P], kv[b:b + HD, 0, 0:n],
                                     start=True, stop=True, skip_group_check=True)
                last.then_inc(sc_ps, 1)

            def turn_probs(s, l):
                bank = 5 + s % 3
                pe.wait_ge(pn_done, HEADS * l + s + 1)
                if s < 3:
                    pe.wait_ge(S_ev, HEADS * (l + 1))
                else:
                    pe.wait_ge(pt_ev, HEADS * l + s - 2)
                for b in range(3):
                    last = pe.transpose(ps[bank][:, b * P:(b + 1) * P], S[:, s, b * P:(b + 1) * P], ident)
                last.then_inc(pt_ps, 1)

            def mix(l):
                t = l * TURNS + MIX_TURN
                v = 3 * l + 1
                ev = l + 1
                split_ready(0, t)
                for ft in range(2):
                    last = up_tile(tiles(0)[:, ft, :], 0, ft, v if ft == 0 else None)
                last.then_inc(unit_done, 1)
                square_sums(v)
                project(M_LR, t, ps[1][0:RANK, 0:SEQ].rearrange("p (a t) -> p a t", a=1), m=RANK)
                spread_r(v)
                project(M_Q0, t, tiles(2))
                pe.wait_ge(kv_ev, ev)
                project(M_Q1, t, tiles(0))
                pe.wait_ge(rb_done, v + 1)
                for tt in range(TT):
                    last = pe.transpose(ps[3][:, tt * P:(tt + 1) * P], kv[:, 1, tt * P:(tt + 1) * P], ident)
                last.then_inc(vt_ps, 1)
                pe.wait_ge(lr_ev, ev)
                pe.wait_ge(s_par, 16 * (l + 1))
                pe.wait_ge(resid_up, 4 * (3 * l + 2))
                for j in range(2):
                    last = pe.matmul(tiles(4)[:, j, :], par[0:RANK, G_UP + j * P:G_UP + (j + 1) * P], glr[:, :],
                                     start=True, stop=True, skip_group_check=True)
                last.then_inc(logit_ps, 1)
                project(M_QG, t, tiles(1))
                pe.wait_ge(q_ev, 2 * l + 1)
                for s in range(4):
                    scores(s, l)
                project(M_KG, t, tiles(2))
                pe.wait_ge(q_ev, 2 * l + 2)
                for s in range(4, HEADS):
                    scores(s, l)
                project_tokens(M_V0, t, tiles(0))
                pe.wait_ge(z_ev, 2 * ev)
                pe.wait_ge(kend_done, ev)
                for j in range(2):
                    for tt in range(TT):
                        last = pe.transpose(ps[4][:, (2 * j + tt) * P:(2 * j + tt + 1) * P],
                                            kend[:, j, tt * P:(tt + 1) * P], ident)
                last.then_inc(ket_ps, 1)
                pe.wait_ge(qg_ev, ev)
                project_tokens(M_V1, t, tiles(1))
                for s in range(4):
                    turn_probs(s, l)
                pe.wait_ge(kg_ev, ev)
                project(M_R0, t, tiles(2))
                for s in range(4, HEADS):
                    turn_probs(s, l)
                pe.wait_ge(ke_done, ev)
                pe.wait_ge(qe_done, ev)
                for h in range(GH):
                    j, b = h // 2, DK * (h % 2)
                    if h == 0:
                        pe.wait_ge(va_ev, ev)
                    if h == 1:
                        pe.wait_ge(ket_ev, ev)
                    for tt in range(TT):
                        c = (2 * j + tt) * P
                        last = pe.matmul(ps[3 + h % 2][:, c:c + P], ke[b:b + DK, j, tt * P:(tt + 1) * P],
                                         qe[b:b + DK, j, tt * P:(tt + 1) * P],
                                         start=True, stop=True, skip_group_check=True)
                    if h >= 2:
                        last.then_inc(A_ps, 1)
                pe.wait_ge(va_ev, ev)
                for j in range(4):
                    bank = (7, 5)[j // 2]
                    pe.wait_ge(pt_ev, HEADS * l + max(2 * j + 2, (6, 7)[j // 2]))
                    for s in (2 * j, 2 * j + 1):
                        b = HD * (s % 2)
                        o = tiles(bank)[b:b + HD, j % 2, :]
                        pe.matmul(o[:, 0:P], va[:, 0, b:b + HD], PT[:, s, 0:P],
                                  start=True, stop=True, skip_group_check=True)
                        pe.matmul(o[:, P:2 * P], va[:, 0, b:b + HD], PT[:, s, P:2 * P],
                                  start=True, stop=False, skip_group_check=True)
                        last = pe.matmul(o[:, P:2 * P], va[:, 1, b:b + HD], PT[:, s, 2 * P:3 * P],
                                         start=False, stop=True, skip_group_check=True)
                    if j % 2:
                        last.then_inc(pv_ps, 1)
                pe.wait_ge(v_ev, 4 * ev)
                pe.wait_ge(pt_ev, HEADS * ev)
                pe.sem_inc(waits_met, 1)
                for c in range(3):
                    if c == 1:
                        pe.wait_ge(A_ev, 2 * ev)
                        pe.sem_inc(waits_met, 1)
                    for h in range(GH):
                        j, b, r = h // 2, DK * (h % 2), CHUNK * (c % 2)
                        o = ps[(6, 4, 6)[c]][b:b + DK, (c // 2 * 2 + j) * P:(c // 2 * 2 + j + 1) * P]
                        last = pe.matmul(o, ket[r:r + CHUNK, 2 * j + c // 2, b:b + DK],
                                         vg[r:r + CHUNK, c // 2, h * P:(h + 1) * P],
                                         start=True, stop=True, skip_group_check=True)
                last.then_inc(upd_ps, 1)
                pe.wait_ge(v_ev, 4 * l + 2)
                project(M_R1, t, tiles(0))
                pe.wait_ge(A_ev, 2 * ev)
                pe.wait_ge(asum_done, ev)
                for tt in range(TT):
                    last = pe.matmul(ps[3][:, tt:tt + 1], sqsum_a[:, tt * P:(tt + 1) * P], ones[:, 0:1],
                                     start=True, stop=True, skip_group_check=True)
                last.then_inc(ass_done, 1)
                pe.wait_ge(rg_ev, 2 * l + 1)
                pe.wait_ge(v_ev, 4 * ev)
                pe.wait_ge(st_done, 5 * ev)
                for h in range(GH):
                    j, b = h // 2, DK * (h % 2)
                    o = tiles(1 + h % 2)[:, h // 2, :]
                    for tt in range(TT):
                        pe.matmul(o[:, tt * P:(tt + 1) * P], vg[:, tt, h * P:(h + 1) * P], AT[:, 4 * (h % 2) + 2 * j + tt, :],
                                  start=(h < 2 and tt == 0), stop=False, skip_group_check=True)
                        for c in (2 * tt, 2 * tt + 1):
                            if c:
                                last = pe.matmul(o[:, c * CHUNK:(c + 1) * CHUNK], Sta[b:b + DK, c - 1, j, :],
                                                 qe[b:b + DK, j, c * CHUNK:(c + 1) * CHUNK],
                                                 start=False, stop=True, skip_group_check=True)
                    if h >= 2:
                        last.then_inc(o_ps, 1)
                pe.wait_ge(adiag_done, ev)
                pe.matmul(ps[3][:, 256:512], ones[:, :], diag[:, 0:2, :].rearrange("p a b -> p (a b)"),
                          start=True, stop=True, skip_group_check=True).then_inc(rA_ps, 1)
                pe.wait_ge(at_ev, 2 * ev)
                for i in range(M_WO, MU - 1):
                    slot, turn = i % 3, t + i // 3
                    split_ready(slot, turn)
                    ks = WO_K[i - M_WO]
                    if ks[0] < 4:
                        pe.wait_ge(mlo_done, 4 * l + 1 + ks[0] // 2)
                    else:
                        pe.wait_ge(mlo_done, 4 * l + 3)
                    for n, k in enumerate(ks):
                        for m in range(KT):
                            w_hi, w_lo = weights(slot, n, D, m * P, P)
                            last = three(acc[m // 2][:, m % 2, :], w_hi, w_lo, xhi[:, k, :], xlo[:, k, :],
                                         k == 0 and m % 2 == 0, False)
                    last.then_inc(unit_done, 1)
                    if i == M_WO:
                        pe.wait_ge(rg_ev, 2 * ev)
                        pe.wait_ge(osq_done, 2 * ev)
                        for h in range(GH):
                            for tt in range(TT):
                                last = pe.matmul(ps[0][:, 2 * h + tt:2 * h + tt + 1],
                                                 sq[:, 4 + h, tt * P:(tt + 1) * P], ones[:, 0:1],
                                                 start=True, stop=True, skip_group_check=True)
                        last.then_inc(oss_done, 1)
                    if i == M_WO + 1:
                        pe.wait_ge(o_ev, 2 * ev)
                        pe.wait_ge(odiag_done, ev)
                        for b in range(2):
                            last = pe.matmul(ps[1 + b][:, :], ones[:, :],
                                             diag[:, 4 * b:4 * b + 4, :].rearrange("p a b -> p (a b)"),
                                             start=True, stop=True, skip_group_check=True)
                        last.then_inc(rG_ps, 1)
                pe.wait_ge(mlo_done, 4 * ev)
                i, ks = MU - 1, WO_K[-1]
                finish(i % 3, t + i // 3, D, [xhi[:, k, :] for k in ks], [xlo[:, k, :] for k in ks], True)

            pe.wait_ge(s_cst, 16)
            pe.sem_inc(unit_done, ST)
            pe.wait_ge(s_set, 3)
            with pe.Fori(0, DEPTH) as l:
                ffn(0, l)
                mix(l)
                ffn(1, l)
            square_sums(3 * DEPTH)
            spread_r(3 * DEPTH)

        @block.scalar
        def _(act):
            def split_hi(slot, turn, width=SLOT, first=False, halves=False):
                act.wait_ge(loaded[slot], 16 * (turn + 1))
                if not first:
                    act.wait_ge(unit_done, ST + 3 * turn + slot - 2)
                r, h, _ = split_views(slot, width, halves)
                nc.scalar.activation(h, r, ACT.Copy).then_inc(hi_done, 1)

            def gains(v, gain):
                for p in range(KT // 2):
                    act.wait_ge(resid_up, 4 * v + p + 1)
                    for m in (2 * p, 2 * p + 1):
                        nc.scalar.activation(xhi[:, m, :], resid[:, m, :], ACT.Copy,
                                             scale=gain[:, m:m + 1]).then_inc(xhi_done, 1)
                    nc.scalar.activation(sq[:, 2 * p:2 * p + 2, :], resid[:, 2 * p:2 * p + 2, :],
                                         ACT.Square).then_inc(sq_done, 1)

            def silu(n):
                act.wait_ge(a_done, n + 1)
                nc.scalar.activation(s32[:, :, :], a32[:, :, :], ACT.Silu).then_inc(silu_done, 1)

            def h_hi(hb, n, turn=None):
                act.wait_ge(h_done, n + 1)
                if turn is not None:
                    act.wait_ge(unit_done, ST + 3 * turn + 2)
                nc.scalar.activation(hhi[hb][:, :, :], h32[:, :, :], ACT.Copy).then_inc(hhi_done, 1)

            def ffn(f, l, after):
                t = l * TURNS + FFN_TURN[f]
                grp = (2 * l + f) * GROUPS
                split_hi(2, t)
                silu(grp)
                split_hi(0, t + 1)
                h_hi(0, grp)
                split_hi(1, t + 1)
                with act.Fori(1, GROUPS - 1) as g:
                    split_hi(2, t + g)
                    silu(grp + g)
                    split_hi(0, t + g + 1)
                    h_hi(0, grp + g, t + g)
                    split_hi(1, t + g + 1)
                g = GROUPS - 1
                split_hi(2, t + g)
                silu(grp + g)
                h_hi(1, grp + g)
                after()

            def mix(l):
                t = l * TURNS + MIX_TURN
                ev = l + 1

                def split_mix(i):
                    if i in PAIRED:
                        act.wait_ge(half_loaded, 16 * (len(PAIRED) * l + PAIRED.index(i) + 1))
                    split_hi(i % 3, t + i // 3, WIDTH[i], halves=i in (M_Q0, M_Q1))

                split_mix(2)
                split_mix(3)
                split_mix(4)
                split_mix(5)
                act.wait_ge(vt_ps, ev)
                nc.scalar.copy(va[:, :, :].rearrange("p a b -> p (a b)"), ps[3][:, 0:2 * P]).then_inc(va_ev, 1)
                act.wait_ge(logit_ps, ev)
                for j in range(2):
                    nc.scalar.activation(z[:, j, :], tiles(4)[:, j, :], ACT.Identity,
                                         bias=par[:, G_BIAS + j:G_BIAS + j + 1]).then_inc(z_ev, 1)
                act.wait_ge(z_ev, 2 * ev)
                nc.scalar.activation(az[:, :, :], z[:, :, :], ACT.Abs).then_inc(gate_act, 1)
                act.wait_ge(gate_act, 2 * l + 1)
                nc.scalar.activation(az[:, :, :], az[:, :, :], ACT.Exp, scale=-1.0).then_inc(gate_act, 1)
                act.wait_ge(gate_act, 2 * l + 2)
                nc.scalar.activation(az[:, :, :], az[:, :, :], ACT.Ln, bias=1.0).then_inc(lg_done, 1)
                split_mix(6)
                act.wait_ge(b_done, 2 * ev)
                nc.scalar.activation(eb[:, :, :], bb[:, :, :], ACT.Exp, scale=1.0 / TAU).then_inc(eb_done, 1)
                nc.scalar.activation(enb[:, :, :], bb[:, :, :], ACT.Exp, scale=-1.0 / TAU).then_inc(enb_done, 1)
                act.wait_ge(bd_done, ev)
                nc.scalar.activation(bd[:, :, :], bd[:, :, :], ACT.Exp, scale=1.0 / TAU).then_inc(eend_done, 1)
                split_mix(7)

                def exps(half):
                    act.wait_ge(nm_done, 2 * l + half + 1)
                    for s in range(4 * half, 4 * half + 4):
                        for tt, (a, n) in enumerate(((0, P), (P, SEQ))):
                            e = nc.scalar.activation(S[:, s, a:a + n], S[:, s, a:a + n], ACT.Exp,
                                                     bias=nm[:, s, tt:tt + 1], accum_out=L[:, s, tt:tt + 1])
                        e.then_inc(exp_done, 1)
                    act.wait_ge(ds_done, 2 * l + half + 1)
                    nc.scalar.activation(es[:, 4 * half:4 * half + 4, :], ds[:, 4 * half:4 * half + 4, :],
                                         ACT.Exp).then_inc(es_done, 1)

                exps(0)
                split_mix(8)
                exps(1)
                act.wait_ge(ket_ps, ev)
                nc.scalar.copy(ket[:, :, :].rearrange("p a b -> p (a b)"), ps[4][:, :]).then_inc(ket_ev, 1)

                def v_out(i, bank):
                    act.wait_ge(unit_done, ST + 3 * t + i + 1)
                    act.wait_ge(rcol_done, ev)
                    for tt in range(TT):
                        nc.scalar.activation(vg[:, tt, (i - M_V0) * UC:(i - M_V0 + 1) * UC], tiles(bank)[:, tt, :],
                                             ACT.Copy, scale=rcol[:, tt:tt + 1]).then_inc(v_ev, 1)

                def probs_out(s):
                    act.wait_ge(pt_ps, HEADS * l + s + 1)
                    nc.scalar.copy(PT[:, s, :], ps[5 + s % 3][:, 0:3 * P]).then_inc(pt_ev, 1)

                v_out(M_V0, 0)
                split_mix(9)
                v_out(M_V1, 1)
                for s in range(4):
                    probs_out(s)
                split_mix(10)
                for s in range(4, HEADS):
                    probs_out(s)
                for b in range(2):
                    act.wait_ge(pv_ps, 2 * l + b + 1)
                    nc.scalar.copy(at32[:, 2 * b:2 * b + 2, :], tiles((7, 5)[b])).then_inc(at_ev, 1)
                    act.wait_ge(at_ev, 2 * l + b + 1)
                    nc.scalar.activation(sq[:, 2 * b:2 * b + 2, :], at32[:, 2 * b:2 * b + 2, :],
                                         ACT.Square).then_inc(asq_done, 1)
                split_mix(11)
                act.wait_ge(rg_ev, 2 * l + 1)
                nc.scalar.activation(sg[:, 0:2, :], sg[:, 0:2, :], ACT.Silu).then_inc(sg_done, 1)
                split_mix(12)
                act.wait_ge(rg_ev, 2 * ev)
                nc.scalar.activation(sg[:, 2:4, :], sg[:, 2:4, :], ACT.Silu).then_inc(sg_done, 1)

                def mixed_hi(b, src):
                    nc.scalar.activation(xhi[:, 2 * b:2 * b + 2, :], src, ACT.Copy).then_inc(mhi_done, 1)

                for b in range(2):
                    act.wait_ge(o_ps, 2 * l + b + 1)
                    nc.scalar.copy(o32[:, b:4:2, :], tiles(1 + b)).then_inc(o_ev, 1)
                for b in range(2):
                    act.wait_ge(am_done, 4 * l + b + 1)
                    mixed_hi(b, at32[:, 2 * b:2 * b + 2, :])
                for b in range(2):
                    act.wait_ge(o_ev, 2 * l + b + 1)
                    nc.scalar.activation(sq[:, 4 + b:8:2, :], o32[:, b:4:2, :],
                                         ACT.Square).then_inc(osq_done, 1)
                split_mix(13)
                for b in range(2):
                    act.wait_ge(am_done, 4 * l + b + 3)
                    mixed_hi(2 + b, o32[:, 2 * b:2 * b + 2, :])
                split_mix(14)

            act.wait_ge(s_gain0, 16)
            gains(0, gain0)
            split_hi(0, 0, first=True)
            split_hi(1, 0, first=True)
            with act.Fori(0, DEPTH) as l:
                t0 = l * TURNS

                def to_mixer():
                    split_hi(0, t0 + MIX_TURN, WIDTH[0])
                    act.wait_ge(s_par, 16 * (l + 1))
                    gains(3 * l + 1, par[:, G_MIX:G_MIX + KT])
                    split_hi(1, t0 + MIX_TURN, WIDTH[1])

                ffn(0, l, to_mixer)
                mix(l)
                t1 = t0 + FFN_TURN[1]
                split_hi(0, t1)
                gains(3 * l + 2, par[:, G_FFN2:G_FFN2 + KT])
                split_hi(1, t1)

                def to_next():
                    with act.If(l < DEPTH - 1):
                        split_hi(0, t0 + TURNS)
                    gains(3 * l + 3, par[:, G_NEXT:G_NEXT + KT])
                    with act.If(l < DEPTH - 1):
                        split_hi(1, t0 + TURNS)

                ffn(1, l, to_next)

        @block.vector
        def _(dve):
            def split_lo(slot, turn, width=SLOT, halves=False):
                dve.wait_ge(hi_done, 3 * turn + slot + 1)
                r, h, lo = split_views(slot, width, halves)
                nc.vector.tensor_tensor(lo, r, h.bitcast(F32), ALU.subtract).then_inc(lo_done, 1)

            def gain_lo(v, m, gain):
                dve.wait_ge(xhi_done, KT * v + m + 1)
                nc.vector.scalar_tensor_tensor(out=xlo[:, m, :], in0=resid[:, m, :], scalar=gain[:, m:m + 1],
                                               in1=xhi[:, m, :].bitcast(F32), op0=ALU.mult, op1=ALU.subtract
                                               ).then_inc(xlo_done, 1)

            def residual(v, last_unit, scale, gain):
                for p in range(KT // 2):
                    if p < 3:
                        dve.wait_ge(acc_pair, 3 * (v - 1) + p + 1)
                    else:
                        dve.wait_ge(unit_done, ST + last_unit + 1)
                    x = resid[:, 2 * p:2 * p + 2, :]
                    nc.vector.scalar_tensor_tensor(out=x, in0=acc[p], scalar=scale, in1=x,
                                                   op0=ALU.mult, op1=ALU.add).then_inc(resid_up, 1)
                    if p:
                        gain_lo(v, 2 * p - 2, gain)
                        gain_lo(v, 2 * p - 1, gain)
                gain_lo(v, KT - 2, gain)
                gain_lo(v, KT - 1, gain)

            def rsqrt(call, sums, n, count):
                base = RS * call
                v, t, a, y = rs_v[:, 0:n], rs_t[:, 0:n], rs_a[:, 0:n], rs_y[:, 0:n]

                def then(k, ins):
                    ins.then_inc(rs_step, 1)
                    dve.wait_ge(rs_step, base + k)

                then(1, nc.vector.tensor_scalar(v, sums, 1.0 / count, EPS, ALU.mult, ALU.add))
                then(2, nc.vector.tensor_scalar(t, v.bitcast(I32), 1, None, ALU.logical_shift_right))
                then(3, nc.vector.tensor_scalar(y.bitcast(I32), t, -1.0, MAGIC, ALU.mult, ALU.add))
                for k in (4, 7, 10):
                    then(k, nc.vector.tensor_tensor(a, y, y, ALU.mult))
                    then(k + 1, nc.vector.scalar_tensor_tensor(out=a, in0=a, scalar=-0.5, in1=v,
                                                               op0=ALU.mult, op1=ALU.mult))
                    then(k + 2, nc.vector.scalar_tensor_tensor(out=y, in0=a, scalar=1.5, in1=y,
                                                               op0=ALU.add, op1=ALU.mult))

            def diagonals(n):
                return nc.vector.tensor_tensor(
                    diag[:, 0:n, :], ident.unsqueeze(1).to_broadcast([P, n, P]),
                    rs_y[:, 0:n].unsqueeze(2).to_broadcast([P, n, P]), ALU.mult)

            def norm_r(v, call):
                dve.wait_ge(ss_done, v + 1)
                rsqrt(call, ps[3][:, 0:TT], TT, D)
                diagonals(TT).then_inc(diag_done, 1)

            def norm_b(v):
                dve.wait_ge(rb_ps, v + 1)
                nc.vector.tensor_copy(rB[:, :], ps[3][:, 256:512]).then_inc(rb_done, 1)

            def r_tiles(n):
                return rB[:, :].unsqueeze(1).to_broadcast([P, n, SEQ])

            def gate_out(n, unit):
                dve.wait_ge(unit_done, ST + unit + 1)
                nc.vector.tensor_tensor(a32[:, :, :], tiles(0), r_tiles(2), ALU.mult).then_inc(a_done, 1)

            def up_out(n, unit):
                dve.wait_ge(unit_done, ST + unit + 1)
                nc.vector.tensor_tensor(u32[:, :, :], tiles(1), r_tiles(2), ALU.mult).then_inc(u_done, 1)
                dve.wait_ge(u_done, n + 1)
                dve.wait_ge(silu_done, n + 1)
                nc.vector.tensor_tensor(h32[:, :, :], s32[:, :, :], u32[:, :, :], ALU.mult).then_inc(h_done, 1)

            def h_lo(hb, n):
                dve.wait_ge(hhi_done, n + 1)
                nc.vector.tensor_tensor(hlo[hb][:, :, :], h32[:, :, :], hhi[hb][:, :, :].bitcast(F32),
                                        ALU.subtract).then_inc(hlo_done, 1)

            def ffn(f, l, v, after):
                t = l * TURNS + FFN_TURN[f]
                grp = (2 * l + f) * GROUPS
                split_lo(2, t)
                norm_r(v, 5 * l + 4 * f)
                norm_b(v)
                dve.wait_ge(rb_done, v + 1)
                gate_out(grp, 3 * t)
                split_lo(0, t + 1)
                up_out(grp, 3 * t + 1)
                h_lo(0, grp)
                split_lo(1, t + 1)
                with dve.Fori(1, GROUPS - 1) as g:
                    split_lo(2, t + g)
                    gate_out(grp + g, 3 * (t + g) - 1)
                    split_lo(0, t + g + 1)
                    up_out(grp + g, 3 * (t + g))
                    h_lo(0, grp + g)
                    split_lo(1, t + g + 1)
                g = GROUPS - 1
                split_lo(2, t + g)
                gate_out(grp + g, 3 * (t + g) - 1)
                up_out(grp + g, 3 * (t + g))
                h_lo(1, grp + g)
                after()

            def mix(l):
                t = l * TURNS + MIX_TURN
                v = 3 * l + 1
                ev = l + 1

                def split_mix(i):
                    split_lo(i % 3, t + i // 3, WIDTH[i], halves=i in (M_Q0, M_Q1))

                def done(i):
                    dve.wait_ge(unit_done, ST + 3 * t + i + 1)

                split_mix(2)
                norm_r(v, 5 * l + 1)
                nc.vector.tensor_copy(rcol[:, :], rs_y[:, 0:TT]).then_inc(rcol_done, 1)
                split_mix(3)
                norm_b(v)
                dve.wait_ge(rb_done, v + 1)
                done(M_KV)
                nc.vector.tensor_tensor(kv[:, :, :], tiles(0), r_tiles(2), ALU.mult).then_inc(kv_ev, 1)
                done(M_LR)
                nc.vector.tensor_tensor(glr[:, :], ps[1][0:RANK, 0:SEQ], rB[0:RANK, :], ALU.mult).then_inc(lr_ev, 1)
                split_mix(4)

                def q_out(half, bank):
                    nc.vector.scalar_tensor_tensor(out=qT[:, 2 * half:2 * half + 2, :], in0=tiles(bank),
                                                   scalar=HD ** -0.5, in1=r_tiles(2), op0=ALU.mult, op1=ALU.mult
                                                   ).then_inc(q_ev, 1)

                done(M_Q0)
                q_out(0, 2)
                split_mix(5)
                done(M_Q1)
                q_out(1, 0)
                dve.wait_ge(lg_done, ev)
                nc.vector.scalar_tensor_tensor(out=la[:, :, :], in0=z[:, :, :], scalar=0.0, in1=az[:, :, :],
                                               op0=ALU.min, op1=ALU.subtract).then_inc(la_done, 1)
                dve.wait_ge(la_done, ev)
                for j in range(2):
                    nc.vector.tensor_tensor_scan(bb[:, j, :], keep[:, :], la[:, j, :], 0.0,
                                                 ALU.mult, ALU.add).then_inc(b_done, 1)
                dve.wait_ge(b_done, 2 * ev)
                for j in range(2):
                    b4 = bb[:, j, :].rearrange("p (c t) -> p c t", c=NCH)
                    d = nc.vector.tensor_tensor(bd[:, j, :].rearrange("p (c t) -> p c t", c=NCH),
                                                b4[:, :, CHUNK - 1:CHUNK].to_broadcast([P, NCH, CHUNK]), b4,
                                                ALU.subtract)
                d.then_inc(bd_done, 1)
                split_mix(6)

                def biased(s):
                    dve.wait_ge(sc_ps, HEADS * l + s + 1)
                    nc.vector.scalar_tensor_tensor(out=S[:, s, :], in0=dist, scalar=2.0 ** -(head(s) + 1),
                                                   in1=ps[5 + s % 3][:, 0:3 * P], op0=ALU.mult, op1=ALU.add
                                                   ).then_inc(S_ev, 1)

                sink = par[:, G_SINK:G_SINK + HEADS].unsqueeze(2).to_broadcast([P, HEADS, 2])

                def maxima(half):
                    h = slice(4 * half, 4 * half + 4)
                    n = 2 * l + half
                    dve.wait_ge(S_ev, HEADS * l + 4 * half + 4)
                    for tt, (a, w) in enumerate(((0, P), (P, SEQ))):
                        nc.vector.tensor_reduce(mx[:, h, tt:tt + 1], S[:, h, a:a + w], AX.X, ALU.max
                                                ).then_inc(max_done, 1)
                    dve.wait_ge(max_done, 2 * n + 2)
                    nc.vector.tensor_tensor(mx[:, h, :], mx[:, h, :], sink[:, h, :], ALU.max).then_inc(soft_step, 1)
                    dve.wait_ge(soft_step, n + 1)
                    nc.vector.tensor_scalar(nm[:, h, :], mx[:, h, :], -1.0, None, ALU.mult).then_inc(nm_done, 1)
                    nc.vector.tensor_tensor(ds[:, h, :], sink[:, h, :], mx[:, h, :], ALU.subtract
                                            ).then_inc(ds_done, 1)

                def normalised(half):
                    h = slice(4 * half, 4 * half + 4)
                    n = 2 * l + half
                    dve.wait_ge(es_done, n + 1)
                    nc.vector.tensor_tensor(Lt[:, h, :], L[:, h, :], es[:, h, :], ALU.add).then_inc(inv_step, 1)
                    dve.wait_ge(inv_step, 2 * n + 1)
                    nc.vector.reciprocal(Li[:, h, :], Lt[:, h, :]).then_inc(inv_step, 1)
                    dve.wait_ge(inv_step, 2 * n + 2)
                    for s in range(4 * half, 4 * half + 4):
                        for tt, (a, w) in enumerate(((0, P), (P, SEQ))):
                            e = nc.vector.tensor_scalar(S[:, s, a:a + w], S[:, s, a:a + w], Li[:, s, tt:tt + 1],
                                                        None, ALU.mult)
                        e.then_inc(pn_done, 1)

                done(M_QG)
                nc.vector.scalar_tensor_tensor(out=qe[:, :, :], in0=tiles(1), scalar=DK ** -0.5, in1=r_tiles(2),
                                               op0=ALU.mult, op1=ALU.mult).then_inc(qg_ev, 1)
                for s in range(4):
                    biased(s)
                maxima(0)
                split_mix(7)
                dve.wait_ge(eb_done, ev)
                dve.wait_ge(qg_ev, ev)
                nc.vector.tensor_tensor(qe[:, :, :], qe[:, :, :], eb[:, :, :], ALU.mult).then_inc(qe_done, 1)
                done(M_KG)
                nc.vector.tensor_tensor(kg[:, :, :], tiles(2), r_tiles(2), ALU.mult).then_inc(kg_ev, 1)
                for s in range(4, HEADS):
                    biased(s)
                maxima(1)
                split_mix(8)
                dve.wait_ge(eend_done, ev)
                dve.wait_ge(kg_ev, ev)
                nc.vector.tensor_tensor(kend[:, :, :], kg[:, :, :], bd[:, :, :], ALU.mult).then_inc(kend_done, 1)
                dve.wait_ge(enb_done, ev)
                nc.vector.tensor_tensor(ke[:, :, :], kg[:, :, :], enb[:, :, :], ALU.mult).then_inc(ke_done, 1)
                normalised(0)
                split_mix(9)
                normalised(1)
                split_mix(10)
                for b in range(2):
                    dve.wait_ge(A_ps, 2 * l + b + 1)
                    dve.sem_inc(waits_met, 1)
                    nc.vector.copy_predicated(AT[:, 4 * b:4 * b + 4, :], mask.unsqueeze(1).to_broadcast([P, 4, P]),
                                              ps[3 + b][:, :].rearrange("p (a t) -> p a t", a=4)).then_inc(A_ev, 1)
                dve.wait_ge(upd_ps, ev)
                upd = [ps[(6, 4, 6)[c]][:, c // 2 * 2 * P:(c // 2 + 1) * 2 * P].rearrange("p (j n) -> p j n", j=2)
                       for c in range(3)]
                nc.vector.tensor_copy(Sta[:, 0, :, :], upd[0]).then_inc(st_done, 1)
                for c in (1, 2):
                    dve.wait_ge(st_done, 5 * l + 2 * c - 1)
                    for j in range(2):
                        new = upd[c][:, j, :]
                        last_token = (c + 1) * CHUNK - 1
                        nc.vector.scalar_tensor_tensor(out=Sta[:, c, j, :], in0=Sta[:, c - 1, j, :],
                                                       scalar=eb[:, j, last_token:last_token + 1], in1=new,
                                                       op0=ALU.mult, op1=ALU.add).then_inc(st_done, 1)
                split_mix(11)
                done(M_R0)
                nc.vector.tensor_tensor(sg[:, 0:2, :], tiles(2), r_tiles(2), ALU.mult).then_inc(rg_ev, 1)
                done(M_R1)
                nc.vector.tensor_tensor(sg[:, 2:4, :], tiles(0), r_tiles(2), ALU.mult).then_inc(rg_ev, 1)
                dve.wait_ge(ass_done, ev)
                rsqrt(5 * l + 2, ps[3][:, 0:TT], TT, 512)
                diagonals(TT).then_inc(adiag_done, 1)
                split_mix(12)
                dve.wait_ge(rA_ps, ev)
                for b in range(2):
                    for j in (2 * b, 2 * b + 1):
                        e = nc.vector.scalar_tensor_tensor(out=at32[:, j, :], in0=at32[:, j, :],
                                                           scalar=par[:, G_ATT + j:G_ATT + j + 1],
                                                           in1=ps[3][:, 256:512], op0=ALU.mult, op1=ALU.mult)
                    e.then_inc(am_done, 1)

                def mixed_lo(b, src):
                    dve.wait_ge(mhi_done, 4 * l + b + 1)
                    nc.vector.tensor_tensor(xlo[:, 2 * b:2 * b + 2, :], src,
                                            xhi[:, 2 * b:2 * b + 2, :].bitcast(F32), ALU.subtract
                                            ).then_inc(mlo_done, 1)

                for b in range(2):
                    mixed_lo(b, at32[:, 2 * b:2 * b + 2, :])
                split_mix(13)
                dve.wait_ge(osq_done, 2 * ev)
                dve.wait_ge(sg_done, 2 * ev)
                nc.vector.scalar_tensor_tensor(out=o32[:, :, :].rearrange("p a b -> p (a b)"),
                                               in0=o32[:, :, :].rearrange("p a b -> p (a b)"),
                                               scalar=par[:, G_GLA:G_GLA + 1],
                                               in1=sg[:, :, :].rearrange("p a b -> p (a b)"),
                                               op0=ALU.mult, op1=ALU.mult).then_inc(og_done, 1)
                dve.wait_ge(oss_done, ev)
                rsqrt(5 * l + 3, ps[0][:, 0:8], 8, P)
                diagonals(8).then_inc(odiag_done, 1)
                dve.wait_ge(og_done, ev)
                dve.wait_ge(rG_ps, ev)
                for b in range(2):
                    o = o32[:, 2 * b:2 * b + 2, :]
                    nc.vector.tensor_tensor(o, o, tiles(1 + b), ALU.mult).then_inc(am_done, 1)
                for b in range(2):
                    mixed_lo(2 + b, o32[:, 2 * b:2 * b + 2, :])
                split_mix(14)

            nc.vector.memset(ones[:, :], 1.0).then_inc(s_set, 1)
            nc.vector.memset(AT[:, :, :], 0.0).then_inc(s_set, 1)
            nc.vector.memset(keep[:, :], 1.0).then_inc(s_keep, 1)
            dve.wait_ge(s_keep, 1)
            nc.vector.memset(keep[:, :].rearrange("p (c t) -> p c t", c=NCH)[:, :, 0:1], 0.0).then_inc(s_set, 1)
            dve.wait_ge(s_set, 3)
            for p in range(KT // 2):
                dve.wait_ge(s_x[p], 16)
                dve.sem_inc(resid_up, 1)
            dve.wait_ge(s_cst, 16)
            dve.wait_ge(s_gain0, 16)
            for m in range(KT):
                gain_lo(0, m, gain0)
            split_lo(0, 0)
            split_lo(1, 0)
            with dve.Fori(0, DEPTH) as l:
                t0 = l * TURNS
                t1 = t0 + FFN_TURN[1]

                def to_mixer():
                    split_lo(0, t0 + MIX_TURN, WIDTH[0])
                    dve.wait_ge(s_par, 16 * (l + 1))
                    residual(3 * l + 1, 3 * (t0 + MIX_TURN) - 1, 0.5, par[:, G_MIX:G_MIX + KT])
                    split_lo(1, t0 + MIX_TURN, WIDTH[1])

                def to_next():
                    with dve.If(l < DEPTH - 1):
                        split_lo(0, t0 + TURNS)
                    residual(3 * l + 3, 3 * (t0 + TURNS) - 1, 0.5, par[:, G_NEXT:G_NEXT + KT])
                    with dve.If(l < DEPTH - 1):
                        split_lo(1, t0 + TURNS)

                ffn(0, l, 3 * l, to_mixer)
                mix(l)
                split_lo(0, t1)
                residual(3 * l + 2, 3 * t1 - 1, 1.0, par[:, G_FFN2:G_FFN2 + KT])
                split_lo(1, t1)
                ffn(1, l, 3 * l + 2, to_next)
            v = 3 * DEPTH
            norm_r(v, 5 * DEPTH)
            norm_b(v)
            dve.wait_ge(rb_done, v + 1)
            for m in range(KT):
                e = nc.vector.scalar_tensor_tensor(out=sq[:, m, :], in0=resid[:, m, :],
                                                   scalar=par[:, G_NEXT + m:G_NEXT + m + 1], in1=rB[:, :],
                                                   op0=ALU.mult, op1=ALU.mult)
                if m % 2:
                    e.then_inc(s_fin, 1)

        @block.gpsimd
        def _(pool):
            def add(o, a, b):
                return nc.gpsimd.tensor_tensor(o, a, b, ALU.add)

            def flat(a, b):
                return sq[:, a:b, :].rearrange("p m t -> p (m t)")

            def sum_squares(v, steps):
                pool.wait_ge(sq_done, 4 * v + 1)
                for p in (1, 2, 3):
                    pool.wait_ge(sq_done, 4 * v + p + 1)
                    add(flat(0, 2), flat(0, 2), flat(2 * p, 2 * p + 2)).then_inc(pool_step, 1)
                    pool.wait_ge(pool_step, steps + p)
                add(sqsum[:, :], sq[:, 0, :], sq[:, 1, :]).then_inc(sqsum_done, 1)

            with pool.Fori(0, DEPTH) as l:
                s = 10 * l
                sum_squares(3 * l, s)
                sum_squares(3 * l + 1, s + 3)
                pool.wait_ge(asq_done, 2 * l + 2)
                add(flat(0, 2), flat(0, 2), flat(2, 4)).then_inc(pool_step, 1)
                pool.wait_ge(pool_step, s + 7)
                add(sqsum_a[:, :], sq[:, 0, :], sq[:, 1, :]).then_inc(asum_done, 1)
                sum_squares(3 * l + 2, s + 7)
            sum_squares(3 * DEPTH, 10 * DEPTH)


def _layouts(a):
    import numpy as np

    def tiles(g):
        return np.ascontiguousarray(g.reshape(-1, P).T)

    x = np.ascontiguousarray(a["x"][0].T.reshape(KT, P, SEQ).transpose(1, 0, 2))
    par = np.zeros((DEPTH, P, NPAR), np.float32)
    for l in range(DEPTH):
        par[l, :, G_MIX:G_MIX + KT] = tiles(a["mix_norm"][l])
        par[l, :, G_FFN2:G_FFN2 + KT] = tiles(a["ffn2_norm"][l])
        par[l, :, G_NEXT:G_NEXT + KT] = tiles(a["ffn1_norm"][l + 1] if l + 1 < DEPTH else a["final_norm"])
        att = a["attn_out_norm"][l].reshape(2, 4, HD)
        par[l, :, G_ATT:G_ATT + 4] = att.transpose(0, 2, 1).reshape(P, 4)
        par[l, :, G_BIAS:G_BIAS + 2] = tiles(a["gla_gate_bias"][l])
        par[l, :, G_GLA] = a["gla_out_norm"][l]
        par[l, :, G_SINK:G_SINK + HEADS] = a["attn_sinks"][l][[head(s) for s in range(HEADS)]][None, :]
        par[l, 0:RANK, G_UP:G_UP + 256] = a["gla_gate_up"][l]
    return x, par, tiles(a["ffn1_norm"][0])


def _constants():
    import numpy as np

    c = np.zeros((P, NCST), np.float32)
    for tt, (a, n) in enumerate(((0, P), (P, SEQ))):
        q = tt * P + np.arange(P)[:, None]
        k = np.arange(n)[None, :]
        back = q // CHUNK - k // CHUNK
        c[:, K_DIST + a:K_DIST + a + n] = np.where((back == 0) | (back == 1), -np.abs(q - k), -3e38)
    i = np.arange(P)
    c[:, K_MASK:K_MASK + P] = (i[:, None] // CHUNK == i[None, :] // CHUNK) & (i[:, None] <= i[None, :])
    c[:, K_ID:K_ID + P] = i[:, None] == i[None, :]
    return c


def kernel(**inputs):
    import numpy as np
    import concourse.bacc as bacc
    from concourse.bass_utils import run_bass_kernel_spmd as run

    a = {k: np.asarray(v) for k, v in inputs.items()}
    x, par, gain0 = _layouts(a)
    arrays = {"xt": x, "par": par, "gain0": gain0, "cst": _constants()}
    weights = ["ffn1_w_gate", "ffn2_w_gate", "ffn1_w_up", "ffn2_w_up", "ffn1_w_down", "ffn2_w_down", "w_in", "w_out"]
    for n in weights:
        arrays[n] = np.ascontiguousarray(a[n])
    nc = bacc.Bacc("TRN2", target_bir_lowering=False, num_devices=1)
    ap = {n: nc.dram_tensor(f"in_{n}", v.shape, F32, kind="ExternalInput").ap() for n, v in arrays.items()}
    out = nc.dram_tensor("out_x", (P, KT, SEQ), F32, kind="ExternalOutput").ap()
    w = [ap[n] for n in weights]
    trunk(nc, ap["xt"], ap["par"], ap["gain0"], ap["cst"], w[0:2], w[2:4], w[4:6], w[6], w[7], out)
    r = run(nc, [{f"in_{n}": v for n, v in arrays.items()}], core_ids=[0])
    y = np.asarray(r.results[0]["out_x"])
    return np.ascontiguousarray(y.transpose(1, 0, 2).reshape(D, SEQ).T)[None]
```

```python
from contextlib import ExitStack

import concourse.bass as bass
from concourse import mybir

F32 = mybir.dt.float32
F32R = mybir.dt.float32r
I32 = mybir.dt.int32
ALU = mybir.AluOpType
ACT = mybir.ActivationFunctionType
AX = mybir.AxisListType

P = 128
SEQ = 256
D = 1024
DEPTH = 2
KT = D // P
TT = SEQ // P
FF = 2816
UC = 256
GROUPS = FF // UC
FT = UC // P
CHUNK = 64
NCH = SEQ // CHUNK
HEADS = 8
HD = 64
GH = 4
DK = 64
RANK = 16
TAU = 16.0
EPS = 1e-6
SLOT = KT * UC

C_Q, C_K, C_V = 0, 512, 640
C_QG, C_KG, C_VG, C_LR, C_RG = 768, 1024, 1280, 1792, 1808
IN_COLS = 2320

G_MIX, G_FFN2, G_NEXT = 0, KT, 2 * KT
G_ATT = 3 * KT
G_BIAS = G_ATT + 4
G_GLA = G_BIAS + 2
G_SINK = G_GLA + 1
G_UP = G_SINK + HEADS
NPAR = G_UP + 256

SEEN = 320
K_DIST, K_MASK, K_ID = 0, SEEN, SEEN + P
NCST = K_ID + P

FU = 3 * GROUPS
MU = 15
LU = 2 * FU + MU
FFN_TURN = (0, (FU + MU) // 3)
MIX_TURN = FU // 3
TURNS = LU // 3
PIECES = KT // 2
WIDTH = [KT * UC, KT * RANK] + [KT * UC] * 8 + [D, D, 2 * D, 2 * D, 2 * D]
WO_K = [(0,), (1,), (2, 3), (4, 5), (6, 7)]
(M_KV, M_LR, M_Q0, M_Q1, M_QG, M_KG, M_V0, M_V1, M_R0, M_R1) = range(10)
M_WO = 10
PAIRED = [M_Q0, M_Q1, M_WO, M_WO + 1, M_WO + 2]
BLOCKS = ((1, 64, 192), (0, 256, 128))

ST = 1
WARM = 20
SETS = 4
RS = 12
MAGIC = float(0x5F3759DF)


def head(s):
    return s // 2 + 4 * (s % 2)


def trunk(nc, xt, par_d, gain0_d, cst_d, fg, fu, fd, w_in, w_out, out):
    ctx = ExitStack()
    with ctx:
        def sb(name, shape, dt=F32):
            return ctx.enter_context(nc.sbuf_tensor(name, shape, dt))

        def sem(name):
            return ctx.enter_context(nc.semaphore(name))

        raw = sb("raw", [P, 3, SLOT])
        whi = sb("whi", [P, 3, SLOT], F32R)
        wlo = sb("wlo", [P, 3, SLOT], F32R)
        resid = sb("resid", [P, KT, SEQ])
        xhi = sb("xhi", [P, KT, SEQ], F32R)
        xlo = sb("xlo", [P, KT, SEQ], F32R)
        sq = sb("sq", [P, KT, SEQ])
        sqsum = sb("sqsum", [P, SEQ])
        sqsum_a = sb("sqsum_a", [P, SEQ])
        par = sb("par", [P, NPAR])
        gain0 = sb("gain0", [P, KT])
        cst = sb("cst", [P, NCST])
        ones = sb("ones", [P, P])
        keep = sb("keep", [P, SEQ])
        rs_v = sb("rs_v", [P, 8])
        rs_t = sb("rs_t", [P, 8], I32)
        rs_a = sb("rs_a", [P, 8])
        rs_y = sb("rs_y", [P, 8])
        rcol = sb("rcol", [P, TT])
        diag = sb("diag", [P, 8, P])
        rB = sb("rB", [P, SEQ])
        work = sb("work", [P, 4 * FT, SEQ])
        a32, s32, u32, h32 = (work[:, FT * i:FT * (i + 1), :] for i in range(4))
        hhi = [sb(f"hhi{i}", [P, FT, SEQ], F32R) for i in range(2)]
        hlo = [sb(f"hlo{i}", [P, FT, SEQ], F32R) for i in range(2)]
        kv = sb("kv", [P, 2, SEQ])
        qT = sb("qT", [P, 4, SEQ])
        glr = sb("glr", [RANK, SEQ])
        va = sb("va", [P, TT, P])
        z = sb("z", [P, 2, SEQ])
        az = sb("az", [P, 2, SEQ])
        la = sb("la", [P, 2, SEQ])
        bb = sb("bb", [P, 2, SEQ])
        bd = sb("bd", [P, 2, SEQ])
        eb = sb("eb", [P, 2, SEQ])
        enb = sb("enb", [P, 2, SEQ])
        qe = sb("qe", [P, 2, SEQ])
        kg = sb("kg", [P, 2, SEQ])
        ke = sb("ke", [P, 2, SEQ])
        kend = sb("kend", [P, 2, SEQ])
        ket = sb("ket", [P, 4, P])
        S = sb("S", [P, HEADS, 3 * P])
        PT = sb("PT", [P, HEADS, 3 * P])
        mx = sb("mx", [P, HEADS, 2])
        nm = sb("nm", [P, HEADS, 2])
        ds = sb("ds", [P, HEADS, 2])
        es = sb("es", [P, HEADS, 2])
        L = sb("L", [P, HEADS, 2])
        Lt = sb("Lt", [P, HEADS, 2])
        Li = sb("Li", [P, HEADS, 2])
        vg = sb("vg", [P, TT, 4 * P])
        AT = sb("AT", [P, 8, P])
        Sta = sb("Sta", [P, 3, 2, P])
        sg = sb("sg", [P, 4, SEQ])
        at32 = work[:, 0:4, :]
        o32 = work[:, 4:8, :]

        ps = [ctx.enter_context(nc.psum_tensor(f"ps{i}", [P, 512], F32)) for i in range(8)]
        acc = [ps[4 + i][:, :].rearrange("p (m t) -> p m t", m=2) for i in range(4)]

        def tiles(bank):
            return ps[bank][:, :].rearrange("p (m t) -> p m t", m=2)

        def split_views(slot, width, halves):
            r, h, lo = raw[:, slot, 0:width], whi[:, slot, 0:width], wlo[:, slot, 0:width]
            if halves:
                r = r.rearrange("p (h n c) -> p h n c", h=2, c=HD)
                h, lo = (w.rearrange("p (n h c) -> p h n c", h=2, c=HD) for w in (h, lo))
            return r, h, lo

        ident = cst[:, K_ID:K_ID + P]
        dist = cst[:, K_DIST:K_DIST + SEEN]
        mask = cst[:, K_MASK:K_MASK + P].bitcast(I32)

        loaded = [sem(f"loaded{i}") for i in range(3)]
        waits_met = sem("waits_met")
        half_loaded = sem("half_loaded")
        s_x = [sem(f"x_loaded{p}") for p in range(KT // 2)]
        s_piece = [[sem(f"piece{u}_{p}") if u else s_x[p] for p in range(PIECES)] for u in range(3)]
        hi_piece, lo_piece = sem("hi_piece"), sem("lo_piece")
        s_gain0 = sem("gain0_loaded")
        s_par = sem("par_loaded")
        s_cst = sem("cst_loaded")
        s_set = sem("buffers_set")
        s_keep = sem("keep_set")
        rcol_done = sem("rcol_done")
        hi_done = sem("hi_done")
        lo_done = sem("lo_done")
        unit_done = sem("unit_done")
        acc_pair = sem("acc_pair")
        resid_up = sem("resid_up")
        xhi_done = sem("xhi_done")
        xlo_done = sem("xlo_done")
        sq_done = sem("sq_done")
        pool_step = sem("pool_step")
        sqsum_done = sem("sqsum_done")
        ss_done = sem("ss_done")
        rs_step = sem("rs_step")
        diag_done = sem("diag_done")
        rb_ps = sem("rb_ps")
        rb_done = sem("rb_done")
        a_done, silu_done, u_done, h_done, hhi_done, hlo_done = (
            sem(n) for n in ("a_done", "silu_done", "u_done", "h_done", "hhi_done", "hlo_done"))
        kv_ev, lr_ev, q_ev = sem("kv_ev"), sem("lr_ev"), sem("q_ev")
        vt_ps, va_ev, logit_ps = sem("vt_ps"), sem("va_ev"), sem("logit_ps")
        z_ev, gate_act, lg_done, la_done, b_done, bd_done = (
            sem(n) for n in ("z_ev", "gate_act", "lg_done", "la_done", "b_done", "bd_done"))
        eb_done, enb_done, eend_done = sem("eb_done"), sem("enb_done"), sem("eend_done")
        qg_ev, qe_done, kg_ev, ke_done, kend_done = (
            sem(n) for n in ("qg_ev", "qe_done", "kg_ev", "ke_done", "kend_done"))
        sc_ps, S_ev, max_done, soft_step, nm_done, ds_done = (
            sem(n) for n in ("sc_ps", "S_ev", "max_done", "soft_step", "nm_done", "ds_done"))
        exp_done, es_done, inv_step, pn_done = (
            sem(n) for n in ("exp_done", "es_done", "inv_step", "pn_done"))
        ket_ps, ket_ev, pt_ps, pt_ev, pv_ps, at_ev = (
            sem(n) for n in ("ket_ps", "ket_ev", "pt_ps", "pt_ev", "pv_ps", "at_ev"))
        v_ev, A_ps, A_ev, upd_ps, st_done = (sem(n) for n in ("v_ev", "A_ps", "A_ev", "upd_ps", "st_done"))
        rg_ev, sg_done, o_ps, o_ev, og_done = (sem(n) for n in ("rg_ev", "sg_done", "o_ps", "o_ev", "og_done"))
        asq_done, asum_done, ass_done, adiag_done, rA_ps = (
            sem(n) for n in ("asq_done", "asum_done", "ass_done", "adiag_done", "rA_ps"))
        osq_done, oss_done, odiag_done, rG_ps = (
            sem(n) for n in ("osq_done", "oss_done", "odiag_done", "rG_ps"))
        am_done, mhi_done, mlo_done = sem("am_done"), sem("mhi_done"), sem("mlo_done")
        scaled_done = sem("scaled_done")
        s_fin, s_out = sem("fin"), sem("stored")

        block = ctx.enter_context(nc.Block())

        @block.sync
        def _(sp):
            def load(slot, turn, src, width, shape):
                sp.wait_ge(lo_done, 3 * turn + slot - 2)
                sp.sem_inc(waits_met, 1)
                dst = raw[:, slot, 0:width]
                if shape:
                    dst = dst.rearrange(*shape[0], **shape[1])
                sp.dma_start(dst, src).then_inc(loaded[slot], 16)

            by_k = (("p (k c) -> p k c",), dict(k=KT))
            by_f = (("p (k c) -> p k c",), dict(k=FT))

            def up_unit(w, l, g):
                return w[bass.ds(l, 1), :, bass.ds(g * UC, UC)].rearrange("a (k p) c -> p (a k) c", p=P)

            def down_unit(w, l, g):
                return w[bass.ds(l, 1), bass.ds(g * UC, UC), :].rearrange("a (k p) c -> p (a k) c", p=P)

            def group0(f, l, turn):
                load(0, turn, up_unit(fg[f], l, 0), SLOT, by_k)
                load(1, turn, up_unit(fu[f], l, 0), SLOT, by_k)

            def group(f, l, g, turn):
                load(2, turn + g - 1, up_unit(fg[f], l, g), SLOT, by_k)
                load(0, turn + g, up_unit(fu[f], l, g), SLOT, by_k)
                load(1, turn + g, down_unit(fd[f], l, g - 1), SLOT, by_f)

            for u, (w, c) in enumerate(((fg[0], 0), (fu[0], 0), (fg[0], UC))):
                pieces = w[0, :, c:c + UC].rearrange("(k p) c -> p k c", p=P)
                for p in range(PIECES):
                    two = slice(2 * p, 2 * p + 2)
                    if u == 0:
                        sp.dma_start(resid[:, two, :], xt[:, two, :]).then_inc(s_x[p], 16)
                    if u == 0 and p == 0:
                        sp.dma_start(gain0[:, :], gain0_d).then_inc(s_gain0, 16)
                    sp.dma_start(raw[:, u, :].rearrange("p (k c) -> p k c", k=KT)[:, two, :],
                                 pieces[:, two, :]).then_inc(s_piece[u][p], 16)
                if u == 1:
                    sp.dma_start(cst[:, :], cst_d).then_inc(s_cst, 16)

            with sp.Fori(0, DEPTH) as l:
                t0 = l * TURNS
                load(0, t0 + 1, up_unit(fu[0], l, 1), SLOT, by_k)
                load(1, t0 + 1, down_unit(fd[0], l, 0), SLOT, by_f)
                sp.wait_ge(xlo_done, KT * (3 * l + 1))
                sp.sem_inc(waits_met, 1)
                sp.dma_start(par[:, :], par_d[bass.ds(l, 1), :, :].rearrange("a p n -> p (a n)")).then_inc(s_par, 16)
                with sp.Fori(2, GROUPS) as g:
                    group(0, l, g, t0)
                load(2, t0 + GROUPS - 1, down_unit(fd[0], l, GROUPS - 1), SLOT, by_f)

                tm = t0 + MIX_TURN
                wi = w_in[bass.ds(l, 1), :, :].rearrange("a (k p) c -> p (a k) c", p=P)
                cols = {M_KV: C_K, M_LR: C_LR, M_QG: C_QG, M_KG: C_KG, M_V0: C_VG, M_V1: C_VG + UC,
                        M_R0: C_RG, M_R1: C_RG + UC}
                for i in range(MU):
                    if i in cols:
                        n = WIDTH[i] // KT
                        src, shape = wi[:, :, cols[i]:cols[i] + n], by_k
                    elif i in PAIRED:
                        if i in (M_Q0, M_Q1):
                            c = C_Q + (i - M_Q0) * P
                            dst = raw[:, i % 3, :].rearrange("p (h k c) -> p h k c", h=2, k=KT)
                            halves = [(dst[:, h], wi[:, :, c + h * 4 * HD:c + h * 4 * HD + P]) for h in range(2)]
                        else:
                            ks = WO_K[i - M_WO]
                            wo = w_out[bass.ds(l, 1), 0:512, :].rearrange("a (h j p) c -> h p (a j) c", h=2, p=HD)
                            halves = [(raw[HD * h:HD * h + HD, i % 3, 0:WIDTH[i]].rearrange(
                                "p (k c) -> p k c", k=len(ks)), wo[h, :, ks[0]:ks[-1] + 1, :]) for h in range(2)]
                        sp.wait_ge(lo_done, 3 * (tm + i // 3) + i % 3 - 2)
                        sp.sem_inc(waits_met, 1)
                        sp.dma_start(*halves[0]).then_inc(half_loaded, 16)
                        sp.dma_start(*halves[1]).then_inc(loaded[i % 3], 16)
                        continue
                    else:
                        ks = WO_K[i - M_WO]
                        shape = (("p (k c) -> p k c",), dict(k=len(ks)))
                        src = w_out[bass.ds(l, 1), ks[0] * P:(ks[-1] + 1) * P, :].rearrange(
                            "a (k p) c -> p (a k) c", p=P)
                    load(i % 3, tm + i // 3, src, WIDTH[i], shape)

                t1 = t0 + FFN_TURN[1]
                group0(1, l, t1)
                with sp.Fori(1, GROUPS) as g:
                    group(1, l, g, t1)
                load(2, t1 + GROUPS - 1, down_unit(fd[1], l, GROUPS - 1), SLOT, by_f)
                with sp.If(l < DEPTH - 1):
                    nxt = nc.s_assert_within(l + 1, 1, DEPTH - 1,
                                             skip_runtime_bounds_check_because="the branch is taken for l < DEPTH - 1")
                    group0(0, nxt, t0 + TURNS)
                    load(2, t0 + TURNS, up_unit(fg[0], nxt, 1), SLOT, by_k)
            for m in range(KT // 2):
                sp.wait_ge(s_fin, m + 1)
                sp.dma_start(out[:, 2 * m:2 * m + 2, :], sq[:, 2 * m:2 * m + 2, :]).then_inc(s_out, 16)
            sp.wait_ge(s_out, 16 * (KT // 2))

        @block.tensor
        def _(pe):
            def three(o, w_hi, w_lo, x_hi, x_lo, start, stop):
                pe.matmul(o, w_hi, x_hi, start=start, stop=False, skip_group_check=True)
                pe.matmul(o, w_hi, x_lo, start=False, stop=False, skip_group_check=True)
                return pe.matmul(o, w_lo, x_hi, start=False, stop=stop, skip_group_check=True)

            def split_ready(slot, turn):
                pe.wait_ge(lo_done, 3 * turn + slot + 1)

            def weights(slot, k, per, a, n):
                return (whi[:, slot, k * per + a:k * per + a + n], wlo[:, slot, k * per + a:k * per + a + n])

            def up_tile(o, slot, ft):
                for k in range(KT):
                    w_hi, w_lo = weights(slot, k, UC, ft * P, P)
                    last = three(o, w_hi, w_lo, xhi[:, k, :], xlo[:, k, :], k == 0, k == KT - 1)
                return last

            def up(slot, turn, bank):
                split_ready(slot, turn)
                for ft in range(FT):
                    last = up_tile(tiles(bank)[:, ft, :], slot, ft)
                last.then_inc(unit_done, 1)

            def down(slot, turn, hb, first):
                split_ready(slot, turn)
                for ft in range(FT):
                    for m in range(KT):
                        w_hi, w_lo = weights(slot, ft, D, m * P, P)
                        last = three(acc[m // 2][:, m % 2, :], w_hi, w_lo, hhi[hb][:, ft, :], hlo[hb][:, ft, :],
                                     first and ft == 0 and m % 2 == 0, False)
                last.then_inc(unit_done, 1)

            def finish(slot, turn, per_k, x_hi, x_lo, pairs):
                split_ready(slot, turn)
                for m in range(KT):
                    for n, (h, lo) in enumerate(zip(x_hi, x_lo)):
                        w_hi, w_lo = weights(slot, n, per_k, m * P, P)
                        last = three(acc[m // 2][:, m % 2, :], w_hi, w_lo, h, lo, False, n == len(x_hi) - 1)
                    if m == KT - 1:
                        last.then_inc(unit_done, 1)
                    elif m % 2:
                        last.then_inc(acc_pair, 1)

            def square_sums(v):
                pe.wait_ge(sqsum_done, v + 1)
                for t in range(TT):
                    last = pe.matmul(ps[3][:, t:t + 1], sqsum[:, t * P:(t + 1) * P], ones[:, 0:1],
                                     start=True, stop=True, skip_group_check=True)
                last.then_inc(ss_done, 1)

            def spread_r(v):
                pe.wait_ge(diag_done, v + 1)
                pe.matmul(ps[3][:, 256:512], ones[:, :], diag[:, 0:2, :].rearrange("p a b -> p (a b)"),
                          start=True, stop=True, skip_group_check=True).then_inc(rb_ps, 1)

            def up_pairs(bank, slot, v):
                for p in range(KT // 2):
                    for ft in range(FT):
                        for k in (2 * p, 2 * p + 1):
                            if ft == 0:
                                pe.wait_ge(xlo_done, KT * v + k + 1)
                            w_hi, w_lo = weights(slot, k, UC, ft * P, P)
                            last = three(tiles(bank)[:, ft, :], w_hi, w_lo, xhi[:, k, :], xlo[:, k, :],
                                         k == 0 and ft == 0, k == KT - 1)
                last.then_inc(unit_done, 1)

            def first_group():
                for u, bank in enumerate((2, 7)):
                    for p in range(PIECES):
                        if p < PIECES - 1:
                            pe.wait_ge(lo_piece, (PIECES - 1) * u + p + 1)
                        else:
                            split_ready(u, 0)
                        for ft in range(FT):
                            for k in (2 * p, 2 * p + 1):
                                if u == 0 and ft == 0:
                                    pe.wait_ge(xlo_done, k + 1)
                                w_hi, w_lo = weights(u, k, UC, ft * P, P)
                                last = three(tiles(bank)[:, ft, :], w_hi, w_lo, xhi[:, k, :], xlo[:, k, :],
                                             k == 0 and ft == 0, k == KT - 1)
                        if u == 1 and p == 1:
                            square_sums(0)
                    last.then_inc(unit_done, 1)

            def begin_ffn(l, v, t):
                split_ready(0, t)
                up_pairs(2, 0, v)
                split_ready(1, t)
                pe.wait_ge(resid_up, 4 * (v + 1))
                up_tile(tiles(7)[:, 0, :], 1, 0)
                square_sums(v)
                up_tile(tiles(7)[:, 1, :], 1, 1).then_inc(unit_done, 1)

            def ffn(f, l):
                t = l * TURNS + FFN_TURN[f]
                v = 3 * l + 2 * f
                grp = (2 * l + f) * GROUPS
                split_ready(2, t)
                up_tile(tiles(0)[:, 0, :], 2, 0)
                spread_r(v)
                up_tile(tiles(0)[:, 1, :], 2, 1).then_inc(unit_done, 1)
                up(0, t + 1, 1)
                pe.wait_ge(hlo_done, grp + 1)
                if f:
                    pe.wait_ge(resid_up, 4 * (3 * l + 3))
                else:
                    pe.wait_ge(resid_up, 4 * (3 * l + 1))
                down(1, t + 1, 0, True)
                with pe.Fori(2, GROUPS) as g:
                    pe.wait_ge(a_done, grp + g)
                    up(2, t + g - 1, 0)
                    pe.wait_ge(u_done, grp + g)
                    up(0, t + g, 1)
                    pe.wait_ge(hlo_done, grp + g)
                    down(1, t + g, 0, False)
                pe.wait_ge(hlo_done, grp + GROUPS)
                finish(2, t + GROUPS - 1, D, [hhi[1][:, i, :] for i in range(FT)],
                       [hlo[1][:, i, :] for i in range(FT)], True)

            def project(i, t, o, between=None, m=P):
                slot, turn = i % 3, t + i // 3
                split_ready(slot, turn)
                per = WIDTH[i] // KT
                for ft in range(max(1, per // P)):
                    for k in range(KT):
                        w_hi, w_lo = weights(slot, k, per, ft * P, m)
                        last = three(o[:, ft, :], w_hi, w_lo, xhi[:, k, :], xlo[:, k, :], k == 0, k == KT - 1)
                    if ft == 0 and between:
                        between()
                last.then_inc(unit_done, 1)

            def project_tokens(i, t, o):
                slot, turn = i % 3, t + i // 3
                split_ready(slot, turn)
                for tt in range(TT):
                    for k in range(KT):
                        w_hi, w_lo = weights(slot, k, UC, 0, UC)
                        x = slice(tt * P, (tt + 1) * P)
                        last = three(o[:, tt, :], xhi[:, k, x], xlo[:, k, x], w_hi, w_lo, k == 0, k == KT - 1)
                last.then_inc(unit_done, 1)

            def scores(s, l):
                j, b, bank = s // 2, HD * (s % 2), 5 + s % 3
                if s == 0:
                    pe.wait_ge(resid_up, 4 * (3 * l + 2))
                if s >= 3:
                    pe.wait_ge(S_ev, HEADS * l + s - 2)
                for t, a, n in BLOCKS:
                    last_key = (t + 1) * P
                    last = pe.matmul(ps[bank][:, a:a + n], qT[b:b + HD, j, t * P:(t + 1) * P],
                                     kv[b:b + HD, 0, last_key - n:last_key],
                                     start=True, stop=True, skip_group_check=True)
                last.then_inc(sc_ps, 1)

            def turn_probs(s, l):
                bank = 5 + s % 3
                pe.wait_ge(pn_done, HEADS * l + s + 1)
                if s < 3:
                    pe.wait_ge(S_ev, HEADS * (l + 1))
                else:
                    pe.wait_ge(pt_ev, HEADS * l + s - 2)
                for b in range(3):
                    last = pe.transpose(ps[bank][:, b * P:(b + 1) * P], S[:, s, b * P:(b + 1) * P], ident)
                last.then_inc(pt_ps, 1)

            def mix(l):
                t = l * TURNS + MIX_TURN
                v = 3 * l + 1
                ev = l + 1
                split_ready(0, t)
                up_pairs(0, 0, v)
                square_sums(v)
                project(M_LR, t, ps[1][0:RANK, 0:SEQ].rearrange("p (a t) -> p a t", a=1), m=RANK)
                project(M_Q0, t, tiles(2), lambda: spread_r(v))
                pe.wait_ge(kv_ev, ev)
                project(M_Q1, t, tiles(0))
                pe.wait_ge(rb_done, v + 1)
                for tt in range(TT):
                    last = pe.transpose(ps[3][:, tt * P:(tt + 1) * P], kv[:, 1, tt * P:(tt + 1) * P], ident)
                last.then_inc(vt_ps, 1)
                pe.wait_ge(lr_ev, ev)
                pe.wait_ge(s_par, 16 * (l + 1))
                pe.wait_ge(resid_up, 4 * (3 * l + 2))
                for j in range(2):
                    last = pe.matmul(tiles(4)[:, j, :], par[0:RANK, G_UP + j * P:G_UP + (j + 1) * P], glr[:, :],
                                     start=True, stop=True, skip_group_check=True)
                last.then_inc(logit_ps, 1)
                project(M_QG, t, tiles(1))
                pe.wait_ge(q_ev, 2 * l + 1)
                for s in range(3):
                    scores(s, l)
                project(M_KG, t, tiles(2))
                pe.wait_ge(q_ev, 2 * l + 2)
                for s in range(3, 6):
                    scores(s, l)
                project_tokens(M_V0, t, tiles(0))
                for s in range(6, HEADS):
                    scores(s, l)
                pe.wait_ge(qg_ev, ev)
                project_tokens(M_V1, t, tiles(1))
                pe.wait_ge(z_ev, 2 * ev)
                pe.wait_ge(kend_done, ev)
                for j in range(2):
                    for tt in range(TT):
                        last = pe.transpose(ps[4][:, (2 * j + tt) * P:(2 * j + tt + 1) * P],
                                            kend[:, j, tt * P:(tt + 1) * P], ident)
                last.then_inc(ket_ps, 1)
                pe.wait_ge(kg_ev, ev)
                project(M_R0, t, tiles(2))
                for s in range(3):
                    turn_probs(s, l)
                pe.wait_ge(ke_done, ev)
                pe.wait_ge(qe_done, ev)
                for h in range(GH):
                    j, b = h // 2, DK * (h % 2)
                    if h == 0:
                        pe.wait_ge(va_ev, ev)
                    if h == 1:
                        pe.wait_ge(ket_ev, ev)
                    for tt in range(TT):
                        c = (2 * j + tt) * P
                        last = pe.matmul(ps[3 + h % 2][:, c:c + P], ke[b:b + DK, j, tt * P:(tt + 1) * P],
                                         qe[b:b + DK, j, tt * P:(tt + 1) * P],
                                         start=True, stop=True, skip_group_check=True)
                    if h >= 2:
                        last.then_inc(A_ps, 1)
                    turn_probs(3 + h, l)
                turn_probs(7, l)
                pe.wait_ge(va_ev, ev)
                for j in range(4):
                    bank = (7, 5)[j // 2]
                    pe.wait_ge(pt_ev, HEADS * l + max(2 * j + 2, (6, 7)[j // 2]))
                    for s in (2 * j, 2 * j + 1):
                        b = HD * (s % 2)
                        o = tiles(bank)[b:b + HD, j % 2, :]
                        pe.matmul(o[:, 0:P], va[:, 0, b:b + HD], PT[:, s, 2 * P:3 * P],
                                  start=True, stop=True, skip_group_check=True)
                        pe.matmul(o[:, P:2 * P], va[:, 0, b:b + HD], PT[:, s, 0:P],
                                  start=True, stop=False, skip_group_check=True)
                        last = pe.matmul(o[:, P:2 * P], va[:, 1, b:b + HD], PT[:, s, P:2 * P],
                                         start=False, stop=True, skip_group_check=True)
                    if j % 2:
                        last.then_inc(pv_ps, 1)
                pe.wait_ge(v_ev, 4 * ev)
                pe.wait_ge(pt_ev, HEADS * ev)
                pe.sem_inc(waits_met, 1)
                for c in range(3):
                    if c == 1:
                        pe.wait_ge(A_ev, 2 * ev)
                        pe.sem_inc(waits_met, 1)
                    for h in range(GH):
                        j, b, r = h // 2, DK * (h % 2), CHUNK * (c % 2)
                        o = ps[(6, 4, 6)[c]][b:b + DK, (c // 2 * 2 + j) * P:(c // 2 * 2 + j + 1) * P]
                        last = pe.matmul(o, ket[r:r + CHUNK, 2 * j + c // 2, b:b + DK],
                                         vg[r:r + CHUNK, c // 2, h * P:(h + 1) * P],
                                         start=True, stop=True, skip_group_check=True)
                last.then_inc(upd_ps, 1)
                pe.wait_ge(v_ev, 4 * l + 2)

                def attention_sums():
                    pe.wait_ge(asum_done, ev)
                    for tt in range(TT):
                        last = pe.matmul(ps[3][:, tt:tt + 1], sqsum_a[:, tt * P:(tt + 1) * P], ones[:, 0:1],
                                         start=True, stop=True, skip_group_check=True)
                    last.then_inc(ass_done, 1)

                project(M_R1, t, tiles(0), attention_sums)
                pe.wait_ge(rg_ev, 2 * l + 1)
                pe.wait_ge(v_ev, 4 * ev)
                pe.wait_ge(st_done, 5 * ev)
                for h in range(GH):
                    j, b = h // 2, DK * (h % 2)
                    o = tiles(1 + h % 2)[:, h // 2, :]
                    for tt in range(TT):
                        pe.matmul(o[:, tt * P:(tt + 1) * P], vg[:, tt, h * P:(h + 1) * P], AT[:, 4 * (h % 2) + 2 * j + tt, :],
                                  start=(h < 2 and tt == 0), stop=False, skip_group_check=True)
                        for c in (2 * tt, 2 * tt + 1):
                            if c:
                                last = pe.matmul(o[:, c * CHUNK:(c + 1) * CHUNK], Sta[b:b + DK, c - 1, j, :],
                                                 qe[b:b + DK, j, c * CHUNK:(c + 1) * CHUNK],
                                                 start=False, stop=True, skip_group_check=True)
                    if h >= 2:
                        last.then_inc(o_ps, 1)
                    if h == 0:
                        pe.wait_ge(adiag_done, ev)
                        pe.matmul(ps[3][:, 256:512], ones[:, :], diag[:, 0:2, :].rearrange("p a b -> p (a b)"),
                                  start=True, stop=True, skip_group_check=True).then_inc(rA_ps, 1)
                pe.wait_ge(at_ev, 2 * ev)
                for i in range(M_WO, MU - 1):
                    slot, turn = i % 3, t + i // 3
                    split_ready(slot, turn)
                    ks = WO_K[i - M_WO]
                    if ks[0] < 4:
                        pe.wait_ge(mlo_done, 4 * l + 1 + ks[0] // 2)
                    else:
                        pe.wait_ge(mlo_done, 4 * l + 3)
                    for n, k in enumerate(ks):
                        for m in range(KT):
                            w_hi, w_lo = weights(slot, n, D, m * P, P)
                            last = three(acc[m // 2][:, m % 2, :], w_hi, w_lo, xhi[:, k, :], xlo[:, k, :],
                                         k == 0 and m % 2 == 0, False)
                        if k == 2:
                            pe.wait_ge(o_ev, 2 * ev)
                            pe.wait_ge(odiag_done, ev)
                            for b in range(2):
                                r = pe.matmul(ps[1 + b][:, :], ones[:, :],
                                              diag[:, 4 * b:4 * b + 4, :].rearrange("p a b -> p (a b)"),
                                              start=True, stop=True, skip_group_check=True)
                            r.then_inc(rG_ps, 1)
                    last.then_inc(unit_done, 1)
                    if i == M_WO:
                        pe.wait_ge(rg_ev, 2 * ev)
                        pe.wait_ge(osq_done, 2 * ev)
                        for h in range(GH):
                            for tt in range(TT):
                                last = pe.matmul(ps[0][:, 2 * h + tt:2 * h + tt + 1],
                                                 sq[:, 4 + h, tt * P:(tt + 1) * P], ones[:, 0:1],
                                                 start=True, stop=True, skip_group_check=True)
                        last.then_inc(oss_done, 1)
                pe.wait_ge(mlo_done, 4 * ev)
                i, ks = MU - 1, WO_K[-1]
                finish(i % 3, t + i // 3, D, [xhi[:, k, :] for k in ks], [xlo[:, k, :] for k in ks], True)

            pe.sem_inc(unit_done, ST)
            pe.wait_ge(s_set, 1)
            for _ in range(WARM):
                pe.matmul(ps[3][:, 0:P], ones[:, :], ones[:, :], start=True, stop=True, skip_group_check=True)
            pe.wait_ge(s_set, SETS)
            first_group()
            pe.wait_ge(s_cst, 16)
            with pe.Fori(0, DEPTH) as l:
                ffn(0, l)
                mix(l)
                begin_ffn(l, 3 * l + 2, l * TURNS + FFN_TURN[1])
                ffn(1, l)
                with pe.If(l < DEPTH - 1):
                    begin_ffn(l, 3 * (l + 1), (l + 1) * TURNS)
            for p in range(1, KT // 2):
                if p == 1:
                    pe.wait_ge(sqsum_done, 3 * DEPTH + 1)
                else:
                    pe.wait_ge(sq_done, 4 * (3 * DEPTH - 1) + p + 1)
                for t in range(TT):
                    for m in (2 * p, 2 * p + 1):
                        last = pe.matmul(ps[3][:, t:t + 1], sq[:, m, t * P:(t + 1) * P], ones[:, 0:1],
                                         start=m == 2 and t == 0, stop=m == KT - 1, skip_group_check=True)
            last.then_inc(ss_done, 1)
            spread_r(3 * DEPTH)

        @block.scalar
        def _(act):
            def split_hi(slot, turn, width=SLOT, halves=False):
                act.wait_ge(loaded[slot], 16 * turn)
                act.wait_ge(unit_done, ST + 3 * turn + slot - 2)
                r, h, _ = split_views(slot, width, halves)
                nc.scalar.activation(h, r, ACT.Copy).then_inc(hi_done, 1)

            def first_hi(u, p):
                act.wait_ge(s_piece[u][p], 16 if u else 32)
                c = slice(2 * p * UC, (2 * p + 2) * UC)
                nc.scalar.activation(whi[:, u, c], raw[:, u, c], ACT.Copy
                                     ).then_inc(hi_piece if p < PIECES - 1 else hi_done, 1)

            def gains(v, gain):
                for p in range(KT // 2):
                    act.wait_ge(resid_up, 4 * v + p + 1)
                    for m in (2 * p, 2 * p + 1):
                        nc.scalar.activation(xhi[:, m, :], resid[:, m, :], ACT.Copy,
                                             scale=gain[:, m:m + 1]).then_inc(xhi_done, 1)
                    nc.scalar.activation(sq[:, 2 * p:2 * p + 2, :], resid[:, 2 * p:2 * p + 2, :],
                                         ACT.Square).then_inc(sq_done, 1)

            def silu(n):
                act.wait_ge(a_done, n + 1)
                nc.scalar.activation(s32[:, :, :], a32[:, :, :], ACT.Silu).then_inc(silu_done, 1)

            def h_hi(hb, n, turn=None):
                act.wait_ge(h_done, n + 1)
                if turn is not None:
                    act.wait_ge(unit_done, ST + 3 * turn + 2)
                nc.scalar.activation(hhi[hb][:, :, :], h32[:, :, :], ACT.Copy).then_inc(hhi_done, 1)

            def ffn(f, l, after):
                t = l * TURNS + FFN_TURN[f]
                grp = (2 * l + f) * GROUPS
                split_hi(0, t + 1)
                split_hi(1, t + 1)
                silu(grp)
                h_hi(0, grp)
                with act.Fori(1, GROUPS - 1) as g:
                    split_hi(2, t + g)
                    silu(grp + g)
                    split_hi(0, t + g + 1)
                    h_hi(0, grp + g, t + g)
                    split_hi(1, t + g + 1)
                g = GROUPS - 1
                split_hi(2, t + g)
                silu(grp + g)
                h_hi(1, grp + g)
                after()

            def mix(l):
                t = l * TURNS + MIX_TURN
                ev = l + 1

                def split_mix(i):
                    if i in PAIRED:
                        act.wait_ge(half_loaded, 16 * (len(PAIRED) * l + PAIRED.index(i) + 1))
                    split_hi(i % 3, t + i // 3, WIDTH[i], halves=i in (M_Q0, M_Q1))

                split_mix(2)
                split_mix(3)
                split_mix(4)
                split_mix(5)
                act.wait_ge(vt_ps, ev)
                nc.scalar.copy(va[:, :, :].rearrange("p a b -> p (a b)"), ps[3][:, 0:2 * P]).then_inc(va_ev, 1)
                act.wait_ge(logit_ps, ev)
                for j in range(2):
                    nc.scalar.activation(z[:, j, :], tiles(4)[:, j, :], ACT.Identity,
                                         bias=par[:, G_BIAS + j:G_BIAS + j + 1]).then_inc(z_ev, 1)
                act.wait_ge(z_ev, 2 * ev)
                nc.scalar.activation(az[:, :, :], z[:, :, :], ACT.Abs).then_inc(gate_act, 1)
                split_mix(6)
                act.wait_ge(gate_act, 2 * l + 1)
                nc.scalar.activation(az[:, :, :], az[:, :, :], ACT.Exp, scale=-1.0).then_inc(gate_act, 1)
                act.wait_ge(gate_act, 2 * l + 2)
                nc.scalar.activation(az[:, :, :], az[:, :, :], ACT.Ln, bias=1.0).then_inc(lg_done, 1)
                split_mix(7)
                act.wait_ge(b_done, 2 * ev)
                nc.scalar.activation(eb[:, :, :], bb[:, :, :], ACT.Exp, scale=1.0 / TAU).then_inc(eb_done, 1)
                nc.scalar.activation(enb[:, :, :], bb[:, :, :], ACT.Exp, scale=-1.0 / TAU).then_inc(enb_done, 1)
                act.wait_ge(bd_done, ev)
                nc.scalar.activation(bd[:, :, :], bd[:, :, :], ACT.Exp, scale=1.0 / TAU).then_inc(eend_done, 1)
                split_mix(8)

                def exps(half):
                    act.wait_ge(nm_done, 2 * l + half + 1)
                    for s in range(4 * half, 4 * half + 4):
                        for tt, a, n in BLOCKS:
                            e = nc.scalar.activation(S[:, s, a:a + n], S[:, s, a:a + n], ACT.Exp,
                                                     bias=nm[:, s, tt:tt + 1], accum_out=L[:, s, tt:tt + 1])
                        e.then_inc(exp_done, 1)
                    act.wait_ge(ds_done, 2 * l + half + 1)
                    nc.scalar.activation(es[:, 4 * half:4 * half + 4, :], ds[:, 4 * half:4 * half + 4, :],
                                         ACT.Exp).then_inc(es_done, 1)

                def v_out(i, bank):
                    act.wait_ge(unit_done, ST + 3 * t + i + 1)
                    act.wait_ge(rcol_done, ev)
                    for tt in range(TT):
                        nc.scalar.activation(vg[:, tt, (i - M_V0) * UC:(i - M_V0 + 1) * UC], tiles(bank)[:, tt, :],
                                             ACT.Copy, scale=rcol[:, tt:tt + 1]).then_inc(v_ev, 1)

                def probs_out(s):
                    act.wait_ge(pt_ps, HEADS * l + s + 1)
                    nc.scalar.copy(PT[:, s, :], ps[5 + s % 3][:, 0:3 * P]).then_inc(pt_ev, 1)

                exps(0)
                v_out(M_V0, 0)
                split_mix(9)
                exps(1)
                v_out(M_V1, 1)
                act.wait_ge(ket_ps, ev)
                nc.scalar.copy(ket[:, :, :].rearrange("p a b -> p (a b)"), ps[4][:, :]).then_inc(ket_ev, 1)
                split_mix(10)
                for s in range(HEADS):
                    probs_out(s)
                for b in range(2):
                    act.wait_ge(pv_ps, 2 * l + b + 1)
                    nc.scalar.copy(at32[:, 2 * b:2 * b + 2, :], tiles((7, 5)[b])).then_inc(at_ev, 1)
                    act.wait_ge(at_ev, 2 * l + b + 1)
                    nc.scalar.activation(sq[:, 2 * b:2 * b + 2, :], at32[:, 2 * b:2 * b + 2, :],
                                         ACT.Square).then_inc(asq_done, 1)
                split_mix(11)
                act.wait_ge(rg_ev, 2 * l + 1)
                nc.scalar.activation(sg[:, 0:2, :], sg[:, 0:2, :], ACT.Silu).then_inc(sg_done, 1)
                split_mix(12)
                act.wait_ge(rg_ev, 2 * ev)
                nc.scalar.activation(sg[:, 2:4, :], sg[:, 2:4, :], ACT.Silu).then_inc(sg_done, 1)

                def mixed_hi(b, src):
                    nc.scalar.activation(xhi[:, 2 * b:2 * b + 2, :], src, ACT.Copy).then_inc(mhi_done, 1)

                for b in range(2):
                    act.wait_ge(am_done, 4 * l + b + 1)
                    mixed_hi(b, at32[:, 2 * b:2 * b + 2, :])
                for b in range(2):
                    act.wait_ge(o_ps, 2 * l + b + 1)
                    nc.scalar.copy(o32[:, b:4:2, :], tiles(1 + b)).then_inc(o_ev, 1)
                    act.wait_ge(o_ev, 2 * l + b + 1)
                    nc.scalar.activation(sq[:, 4 + b:8:2, :], o32[:, b:4:2, :],
                                         ACT.Square).then_inc(osq_done, 1)
                split_mix(13)
                split_mix(14)
                for b in range(2):
                    act.wait_ge(am_done, 4 * l + b + 3)
                    mixed_hi(2 + b, o32[:, 2 * b:2 * b + 2, :])

            act.wait_ge(s_set, SETS)
            nc.scalar.activation(L[:, 0, :], ones[:, 0:2], ACT.Copy).then_inc(waits_met, 1)
            act.wait_ge(s_gain0, 16)
            for p in range(PIECES):
                act.wait_ge(s_x[p], 32)
                for m in (2 * p, 2 * p + 1):
                    nc.scalar.activation(xhi[:, m, :], resid[:, m, :], ACT.Copy,
                                         scale=gain0[:, m:m + 1]).then_inc(xhi_done, 1)
                first_hi(0, p)
            for u in (1, 2):
                for p in range(PIECES):
                    first_hi(u, p)
            with act.Fori(0, DEPTH) as l:
                t0 = l * TURNS

                def to_mixer():
                    split_hi(0, t0 + MIX_TURN, WIDTH[0])
                    split_hi(1, t0 + MIX_TURN, WIDTH[1])
                    act.wait_ge(s_par, 16 * (l + 1))
                    gains(3 * l + 1, par[:, G_MIX:G_MIX + KT])

                ffn(0, l, to_mixer)
                mix(l)
                t1 = t0 + FFN_TURN[1]
                split_hi(0, t1)
                split_hi(1, t1)
                gains(3 * l + 2, par[:, G_FFN2:G_FFN2 + KT])
                split_hi(2, t1)

                def to_next():
                    with act.If(l < DEPTH - 1):
                        split_hi(0, t0 + TURNS)
                        split_hi(1, t0 + TURNS)
                        gains(3 * l + 3, par[:, G_NEXT:G_NEXT + KT])
                        split_hi(2, t0 + TURNS)

                ffn(1, l, to_next)
            v = 3 * DEPTH
            for p in range(KT // 2):
                act.wait_ge(resid_up, 4 * v + p + 1)
                nc.scalar.activation(sq[:, 2 * p:2 * p + 2, :], resid[:, 2 * p:2 * p + 2, :],
                                     ACT.Square).then_inc(sq_done, 1)
            for m in range(KT):
                nc.scalar.activation(work[:, m, :], resid[:, m, :], ACT.Copy,
                                     scale=par[:, G_NEXT + m:G_NEXT + m + 1]).then_inc(scaled_done, 1)

        @block.vector
        def _(dve):
            def split_lo(slot, turn, width=SLOT, halves=False):
                dve.wait_ge(hi_done, 3 * turn + slot + 1)
                r, h, lo = split_views(slot, width, halves)
                nc.vector.tensor_tensor(lo, r, h.bitcast(F32), ALU.subtract).then_inc(lo_done, 1)

            def gain_lo(v, m, gain):
                dve.wait_ge(xhi_done, KT * v + m + 1)
                nc.vector.scalar_tensor_tensor(out=xlo[:, m, :], in0=resid[:, m, :], scalar=gain[:, m:m + 1],
                                               in1=xhi[:, m, :].bitcast(F32), op0=ALU.mult, op1=ALU.subtract
                                               ).then_inc(xlo_done, 1)

            def first_lo(u, p):
                if p < PIECES - 1:
                    dve.wait_ge(hi_piece, (PIECES - 1) * u + p + 1)
                else:
                    dve.wait_ge(hi_done, u + 1)
                c = slice(2 * p * UC, (2 * p + 2) * UC)
                nc.vector.tensor_tensor(wlo[:, u, c], raw[:, u, c], whi[:, u, c].bitcast(F32), ALU.subtract
                                        ).then_inc(lo_piece if p < PIECES - 1 else lo_done, 1)

            def residual(v, last_unit, scale, gain):
                for p in range(KT // 2):
                    if p < 3:
                        dve.wait_ge(acc_pair, 3 * (v - 1) + p + 1)
                    else:
                        dve.wait_ge(unit_done, ST + last_unit + 1)
                    x = resid[:, 2 * p:2 * p + 2, :]
                    nc.vector.scalar_tensor_tensor(out=x, in0=acc[p], scalar=scale, in1=x,
                                                   op0=ALU.mult, op1=ALU.add).then_inc(resid_up, 1)
                    if p and gain is not None:
                        gain_lo(v, 2 * p - 2, gain)
                        gain_lo(v, 2 * p - 1, gain)
                if gain is not None:
                    gain_lo(v, KT - 2, gain)
                    gain_lo(v, KT - 1, gain)

            def rsqrt(call, sums, n, count):
                base = RS * call
                v, t, a, y = rs_v[:, 0:n], rs_t[:, 0:n], rs_a[:, 0:n], rs_y[:, 0:n]

                def then(k, ins):
                    ins.then_inc(rs_step, 1)
                    dve.wait_ge(rs_step, base + k)

                then(1, nc.vector.tensor_scalar(v, sums, 1.0 / count, EPS, ALU.mult, ALU.add))
                then(2, nc.vector.tensor_scalar(t, v.bitcast(I32), 1, None, ALU.logical_shift_right))
                then(3, nc.vector.tensor_scalar(y.bitcast(I32), t, -1.0, MAGIC, ALU.mult, ALU.add))
                for k in (4, 7, 10):
                    then(k, nc.vector.tensor_tensor(a, y, y, ALU.mult))
                    then(k + 1, nc.vector.scalar_tensor_tensor(out=a, in0=a, scalar=-0.5, in1=v,
                                                               op0=ALU.mult, op1=ALU.mult))
                    then(k + 2, nc.vector.scalar_tensor_tensor(out=y, in0=a, scalar=1.5, in1=y,
                                                               op0=ALU.add, op1=ALU.mult))

            def diagonals(n):
                return nc.vector.tensor_tensor(
                    diag[:, 0:n, :], ident.unsqueeze(1).to_broadcast([P, n, P]),
                    rs_y[:, 0:n].unsqueeze(2).to_broadcast([P, n, P]), ALU.mult)

            def norm_r(v, call):
                dve.wait_ge(ss_done, v + 1)
                rsqrt(call, ps[3][:, 0:TT], TT, D)
                diagonals(TT).then_inc(diag_done, 1)

            def norm_b(v):
                dve.wait_ge(rb_ps, v + 1)
                nc.vector.tensor_copy(rB[:, :], ps[3][:, 256:512]).then_inc(rb_done, 1)

            def r_tiles(n):
                return rB[:, :].unsqueeze(1).to_broadcast([P, n, SEQ])

            def gate_out(n, unit, bank=0):
                dve.wait_ge(unit_done, ST + unit + 1)
                nc.vector.tensor_tensor(a32[:, :, :], tiles(bank), r_tiles(2), ALU.mult).then_inc(a_done, 1)

            def up_out(n, unit, bank=1):
                dve.wait_ge(unit_done, ST + unit + 1)
                nc.vector.tensor_tensor(u32[:, :, :], tiles(bank), r_tiles(2), ALU.mult).then_inc(u_done, 1)
                dve.wait_ge(u_done, n + 1)
                dve.wait_ge(silu_done, n + 1)
                nc.vector.tensor_tensor(h32[:, :, :], s32[:, :, :], u32[:, :, :], ALU.mult).then_inc(h_done, 1)

            def h_lo(hb, n):
                dve.wait_ge(hhi_done, n + 1)
                nc.vector.tensor_tensor(hlo[hb][:, :, :], h32[:, :, :], hhi[hb][:, :, :].bitcast(F32),
                                        ALU.subtract).then_inc(hlo_done, 1)

            def ffn(f, l, v, after):
                t = l * TURNS + FFN_TURN[f]
                grp = (2 * l + f) * GROUPS
                norm_r(v, 5 * l + 4 * f)
                split_lo(0, t + 1)
                norm_b(v)
                dve.wait_ge(rb_done, v + 1)
                gate_out(grp, 3 * t, 2)
                up_out(grp, 3 * t + 1, 7)
                split_lo(1, t + 1)
                h_lo(0, grp)
                with dve.Fori(1, GROUPS - 1) as g:
                    split_lo(2, t + g)
                    gate_out(grp + g, 3 * (t + g) - 1)
                    split_lo(0, t + g + 1)
                    up_out(grp + g, 3 * (t + g))
                    h_lo(0, grp + g)
                    split_lo(1, t + g + 1)
                g = GROUPS - 1
                split_lo(2, t + g)
                gate_out(grp + g, 3 * (t + g) - 1)
                up_out(grp + g, 3 * (t + g))
                h_lo(1, grp + g)
                after()

            def mix(l):
                t = l * TURNS + MIX_TURN
                v = 3 * l + 1
                ev = l + 1

                def split_mix(i):
                    split_lo(i % 3, t + i // 3, WIDTH[i], halves=i in (M_Q0, M_Q1))

                def done(i):
                    dve.wait_ge(unit_done, ST + 3 * t + i + 1)

                split_mix(2)
                norm_r(v, 5 * l + 1)
                nc.vector.tensor_copy(rcol[:, :], rs_y[:, 0:TT]).then_inc(rcol_done, 1)
                split_mix(3)
                norm_b(v)
                dve.wait_ge(rb_done, v + 1)
                done(M_KV)
                nc.vector.tensor_tensor(kv[:, :, :], tiles(0), r_tiles(2), ALU.mult).then_inc(kv_ev, 1)
                done(M_LR)
                nc.vector.tensor_tensor(glr[:, :], ps[1][0:RANK, 0:SEQ], rB[0:RANK, :], ALU.mult).then_inc(lr_ev, 1)
                split_mix(4)

                def q_out(half, bank):
                    nc.vector.scalar_tensor_tensor(out=qT[:, 2 * half:2 * half + 2, :], in0=tiles(bank),
                                                   scalar=HD ** -0.5, in1=r_tiles(2), op0=ALU.mult, op1=ALU.mult
                                                   ).then_inc(q_ev, 1)

                done(M_Q0)
                q_out(0, 2)
                split_mix(5)
                done(M_Q1)
                q_out(1, 0)
                split_mix(6)

                def biased(s):
                    dve.wait_ge(sc_ps, HEADS * l + s + 1)
                    nc.vector.scalar_tensor_tensor(out=S[:, s, 64:384], in0=dist, scalar=2.0 ** -(head(s) + 1),
                                                   in1=ps[5 + s % 3][:, 64:384], op0=ALU.mult, op1=ALU.add
                                                   ).then_inc(S_ev, 1)

                for s in range(3):
                    biased(s)
                dve.wait_ge(lg_done, ev)
                nc.vector.scalar_tensor_tensor(out=la[:, :, :], in0=z[:, :, :], scalar=0.0, in1=az[:, :, :],
                                               op0=ALU.min, op1=ALU.subtract).then_inc(la_done, 1)
                dve.wait_ge(la_done, ev)
                for j in range(2):
                    nc.vector.tensor_tensor_scan(bb[:, j, :], keep[:, :], la[:, j, :], 0.0,
                                                 ALU.mult, ALU.add).then_inc(b_done, 1)
                dve.wait_ge(b_done, 2 * ev)
                for j in range(2):
                    b4 = bb[:, j, :].rearrange("p (c t) -> p c t", c=NCH)
                    d = nc.vector.tensor_tensor(bd[:, j, :].rearrange("p (c t) -> p c t", c=NCH),
                                                b4[:, :, CHUNK - 1:CHUNK].to_broadcast([P, NCH, CHUNK]), b4,
                                                ALU.subtract)
                d.then_inc(bd_done, 1)
                split_mix(7)
                sink = par[:, G_SINK:G_SINK + HEADS].unsqueeze(2).to_broadcast([P, HEADS, 2])

                def maxima(half):
                    h = slice(4 * half, 4 * half + 4)
                    n = 2 * l + half
                    dve.wait_ge(S_ev, HEADS * l + 4 * half + 4)
                    for tt, a, w in BLOCKS:
                        nc.vector.tensor_reduce(mx[:, h, tt:tt + 1], S[:, h, a:a + w], AX.X, ALU.max
                                                ).then_inc(max_done, 1)
                    dve.wait_ge(max_done, 2 * n + 2)
                    nc.vector.tensor_tensor(mx[:, h, :], mx[:, h, :], sink[:, h, :], ALU.max).then_inc(soft_step, 1)
                    dve.wait_ge(soft_step, n + 1)
                    nc.vector.tensor_scalar(nm[:, h, :], mx[:, h, :], -1.0, None, ALU.mult).then_inc(nm_done, 1)
                    nc.vector.tensor_tensor(ds[:, h, :], sink[:, h, :], mx[:, h, :], ALU.subtract
                                            ).then_inc(ds_done, 1)

                def normalised(half):
                    h = slice(4 * half, 4 * half + 4)
                    n = 2 * l + half
                    dve.wait_ge(es_done, n + 1)
                    nc.vector.tensor_tensor(Lt[:, h, :], L[:, h, :], es[:, h, :], ALU.add).then_inc(inv_step, 1)
                    dve.wait_ge(inv_step, 2 * n + 1)
                    nc.vector.reciprocal(Li[:, h, :], Lt[:, h, :]).then_inc(inv_step, 1)
                    dve.wait_ge(inv_step, 2 * n + 2)
                    for s in range(4 * half, 4 * half + 4):
                        for tt, a, w in BLOCKS:
                            e = nc.vector.tensor_scalar(S[:, s, a:a + w], S[:, s, a:a + w], Li[:, s, tt:tt + 1],
                                                        None, ALU.mult)
                        e.then_inc(pn_done, 1)

                done(M_QG)
                nc.vector.scalar_tensor_tensor(out=qe[:, :, :], in0=tiles(1), scalar=DK ** -0.5, in1=r_tiles(2),
                                               op0=ALU.mult, op1=ALU.mult).then_inc(qg_ev, 1)
                done(M_KG)
                nc.vector.tensor_tensor(kg[:, :, :], tiles(2), r_tiles(2), ALU.mult).then_inc(kg_ev, 1)
                for s in range(3, 6):
                    biased(s)
                maxima(0)
                dve.wait_ge(eb_done, ev)
                dve.wait_ge(qg_ev, ev)
                nc.vector.tensor_tensor(qe[:, :, :], qe[:, :, :], eb[:, :, :], ALU.mult).then_inc(qe_done, 1)
                dve.wait_ge(eend_done, ev)
                dve.wait_ge(kg_ev, ev)
                nc.vector.tensor_tensor(kend[:, :, :], kg[:, :, :], bd[:, :, :], ALU.mult).then_inc(kend_done, 1)
                dve.wait_ge(enb_done, ev)
                nc.vector.tensor_tensor(ke[:, :, :], kg[:, :, :], enb[:, :, :], ALU.mult).then_inc(ke_done, 1)
                split_mix(8)
                for s in range(6, HEADS):
                    biased(s)
                maxima(1)
                normalised(0)
                split_mix(9)
                normalised(1)
                split_mix(10)
                for b in range(2):
                    dve.wait_ge(A_ps, 2 * l + b + 1)
                    dve.sem_inc(waits_met, 1)
                    nc.vector.copy_predicated(AT[:, 4 * b:4 * b + 4, :], mask.unsqueeze(1).to_broadcast([P, 4, P]),
                                              ps[3 + b][:, :].rearrange("p (a t) -> p a t", a=4)).then_inc(A_ev, 1)
                done(M_R0)
                nc.vector.tensor_tensor(sg[:, 0:2, :], tiles(2), r_tiles(2), ALU.mult).then_inc(rg_ev, 1)
                dve.wait_ge(upd_ps, ev)
                upd = [ps[(6, 4, 6)[c]][:, c // 2 * 2 * P:(c // 2 + 1) * 2 * P].rearrange("p (j n) -> p j n", j=2)
                       for c in range(3)]
                nc.vector.tensor_copy(Sta[:, 0, :, :], upd[0]).then_inc(st_done, 1)
                for c in (1, 2):
                    dve.wait_ge(st_done, 5 * l + 2 * c - 1)
                    for j in range(2):
                        new = upd[c][:, j, :]
                        last_token = (c + 1) * CHUNK - 1
                        nc.vector.scalar_tensor_tensor(out=Sta[:, c, j, :], in0=Sta[:, c - 1, j, :],
                                                       scalar=eb[:, j, last_token:last_token + 1], in1=new,
                                                       op0=ALU.mult, op1=ALU.add).then_inc(st_done, 1)
                split_mix(11)
                dve.wait_ge(ass_done, ev)
                rsqrt(5 * l + 2, ps[3][:, 0:TT], TT, 512)
                diagonals(TT).then_inc(adiag_done, 1)
                done(M_R1)
                nc.vector.tensor_tensor(sg[:, 2:4, :], tiles(0), r_tiles(2), ALU.mult).then_inc(rg_ev, 1)
                dve.wait_ge(rA_ps, ev)
                for b in range(2):
                    for j in (2 * b, 2 * b + 1):
                        e = nc.vector.scalar_tensor_tensor(out=at32[:, j, :], in0=at32[:, j, :],
                                                           scalar=par[:, G_ATT + j:G_ATT + j + 1],
                                                           in1=ps[3][:, 256:512], op0=ALU.mult, op1=ALU.mult)
                    e.then_inc(am_done, 1)

                def mixed_lo(b, src):
                    dve.wait_ge(mhi_done, 4 * l + b + 1)
                    nc.vector.tensor_tensor(xlo[:, 2 * b:2 * b + 2, :], src,
                                            xhi[:, 2 * b:2 * b + 2, :].bitcast(F32), ALU.subtract
                                            ).then_inc(mlo_done, 1)

                for b in range(2):
                    mixed_lo(b, at32[:, 2 * b:2 * b + 2, :])
                split_mix(12)
                dve.wait_ge(osq_done, 2 * ev)
                dve.wait_ge(sg_done, 2 * ev)
                nc.vector.scalar_tensor_tensor(out=o32[:, :, :].rearrange("p a b -> p (a b)"),
                                               in0=o32[:, :, :].rearrange("p a b -> p (a b)"),
                                               scalar=par[:, G_GLA:G_GLA + 1],
                                               in1=sg[:, :, :].rearrange("p a b -> p (a b)"),
                                               op0=ALU.mult, op1=ALU.mult).then_inc(og_done, 1)
                dve.wait_ge(oss_done, ev)
                rsqrt(5 * l + 3, ps[0][:, 0:8], 8, P)
                diagonals(8).then_inc(odiag_done, 1)
                split_mix(13)
                dve.wait_ge(og_done, ev)
                dve.wait_ge(rG_ps, ev)
                for b in range(2):
                    o = o32[:, 2 * b:2 * b + 2, :]
                    nc.vector.tensor_tensor(o, o, tiles(1 + b), ALU.mult).then_inc(am_done, 1)
                for b in range(2):
                    mixed_lo(2 + b, o32[:, 2 * b:2 * b + 2, :])
                split_mix(14)

            nc.vector.memset(ones[:, :], 1.0).then_inc(s_set, 1)
            nc.vector.memset(AT[:, :, :], 0.0).then_inc(s_set, 1)
            nc.vector.memset(keep[:, :], 1.0).then_inc(s_keep, 1)
            dve.wait_ge(s_keep, 1)
            nc.vector.memset(keep[:, :].rearrange("p (c t) -> p c t", c=NCH)[:, :, 0:1], 0.0).then_inc(s_set, 1)
            nc.vector.memset(S[:, :, 0:64], 0.0).then_inc(s_set, 1)
            dve.wait_ge(s_set, SETS)
            dve.wait_ge(s_gain0, 16)
            for p in range(PIECES):
                dve.wait_ge(s_x[p], 32)
                for m in (2 * p, 2 * p + 1):
                    gain_lo(0, m, gain0)
                first_lo(0, p)
            dve.sem_inc(resid_up, KT // 2)
            for u in (1, 2):
                for p in range(PIECES):
                    first_lo(u, p)
            dve.wait_ge(s_cst, 16)
            with dve.Fori(0, DEPTH) as l:
                t0 = l * TURNS
                t1 = t0 + FFN_TURN[1]

                def to_mixer():
                    split_lo(0, t0 + MIX_TURN, WIDTH[0])
                    dve.wait_ge(s_par, 16 * (l + 1))
                    residual(3 * l + 1, 3 * (t0 + MIX_TURN) - 1, 0.5, par[:, G_MIX:G_MIX + KT])
                    split_lo(1, t0 + MIX_TURN, WIDTH[1])

                def to_next():
                    with dve.If(l < DEPTH - 1):
                        split_lo(0, t0 + TURNS)
                        residual(3 * l + 3, 3 * (t0 + TURNS) - 1, 0.5, par[:, G_NEXT:G_NEXT + KT])
                        split_lo(1, t0 + TURNS)
                        split_lo(2, t0 + TURNS)

                ffn(0, l, 3 * l, to_mixer)
                mix(l)
                split_lo(0, t1)
                residual(3 * l + 2, 3 * t1 - 1, 1.0, par[:, G_FFN2:G_FFN2 + KT])
                split_lo(1, t1)
                split_lo(2, t1)
                ffn(1, l, 3 * l + 2, to_next)
            v = 3 * DEPTH
            residual(v, 3 * DEPTH * TURNS - 1, 0.5, None)
            norm_r(v, 5 * DEPTH)
            dve.wait_ge(rb_ps, v + 1)
            dve.wait_ge(scaled_done, KT)
            for p in range(KT // 2):
                nc.vector.tensor_tensor(sq[:, 2 * p:2 * p + 2, :], work[:, 2 * p:2 * p + 2, :],
                                        ps[3][:, 256:512].unsqueeze(1).to_broadcast([P, 2, SEQ]),
                                        ALU.mult).then_inc(s_fin, 1)

        @block.gpsimd
        def _(pool):
            def add(o, a, b):
                return nc.gpsimd.tensor_tensor(o, a, b, ALU.add)

            def flat(a, b):
                return sq[:, a:b, :].rearrange("p m t -> p (m t)")

            def sum_squares(v, steps):
                pool.wait_ge(sq_done, 4 * v - 3)
                for p in (1, 2, 3):
                    pool.wait_ge(sq_done, 4 * v - 3 + p)
                    add(flat(0, 2), flat(0, 2), flat(2 * p, 2 * p + 2)).then_inc(pool_step, 1)
                    pool.wait_ge(pool_step, steps + p)
                add(sqsum[:, :], sq[:, 0, :], sq[:, 1, :]).then_inc(sqsum_done, 1)

            for p in range(KT // 2):
                pool.wait_ge(s_x[p], 32)
                x = resid[:, 2 * p:2 * p + 2, :]
                nc.gpsimd.tensor_tensor(sq[:, 2 * p:2 * p + 2, :], x, x, ALU.mult).then_inc(pool_step, 1)
            for p in (1, 2, 3):
                pool.wait_ge(pool_step, 3 + p)
                add(flat(0, 2), flat(0, 2), flat(2 * p, 2 * p + 2)).then_inc(pool_step, 1)
            pool.wait_ge(pool_step, 7)
            add(sqsum[:, :], sq[:, 0, :], sq[:, 1, :]).then_inc(sqsum_done, 1)
            with pool.Fori(0, DEPTH) as l:
                s = 10 * l + 7
                sum_squares(3 * l + 1, s)
                pool.wait_ge(asq_done, 2 * l + 2)
                add(flat(0, 2), flat(0, 2), flat(2, 4)).then_inc(pool_step, 1)
                pool.wait_ge(pool_step, s + 4)
                add(sqsum_a[:, :], sq[:, 0, :], sq[:, 1, :]).then_inc(asum_done, 1)
                sum_squares(3 * l + 2, s + 4)
                with pool.If(l < DEPTH - 1):
                    sum_squares(3 * l + 3, s + 7)
            pool.wait_ge(sq_done, 4 * (3 * DEPTH - 1) + 2)
            add(flat(2, 4), flat(0, 2), flat(2, 4)).then_inc(sqsum_done, 1)


def _layouts(a):
    import numpy as np

    def tiles(g):
        return np.ascontiguousarray(g.reshape(-1, P).T)

    x = np.ascontiguousarray(a["x"][0].T.reshape(KT, P, SEQ).transpose(1, 0, 2))
    par = np.zeros((DEPTH, P, NPAR), np.float32)
    for l in range(DEPTH):
        par[l, :, G_MIX:G_MIX + KT] = tiles(a["mix_norm"][l])
        par[l, :, G_FFN2:G_FFN2 + KT] = tiles(a["ffn2_norm"][l])
        par[l, :, G_NEXT:G_NEXT + KT] = tiles(a["ffn1_norm"][l + 1] if l + 1 < DEPTH else a["final_norm"])
        att = a["attn_out_norm"][l].reshape(2, 4, HD)
        par[l, :, G_ATT:G_ATT + 4] = att.transpose(0, 2, 1).reshape(P, 4)
        par[l, :, G_BIAS:G_BIAS + 2] = tiles(a["gla_gate_bias"][l])
        par[l, :, G_GLA] = a["gla_out_norm"][l]
        par[l, :, G_SINK:G_SINK + HEADS] = a["attn_sinks"][l][[head(s) for s in range(HEADS)]][None, :]
        par[l, 0:RANK, G_UP:G_UP + 256] = a["gla_gate_up"][l]
    return x, par, tiles(a["ffn1_norm"][0])


def _constants():
    import numpy as np

    c = np.zeros((P, NCST), np.float32)
    for tt, a, n in BLOCKS:
        q = tt * P + np.arange(P)[:, None]
        k = (tt + 1) * P - n + np.arange(n)[None, :]
        back = q // CHUNK - k // CHUNK
        a += K_DIST - BLOCKS[0][1]
        c[:, a:a + n] = np.where((back == 0) | (back == 1), -np.abs(q - k), -3e38)
    i = np.arange(P)
    c[:, K_MASK:K_MASK + P] = (i[:, None] // CHUNK == i[None, :] // CHUNK) & (i[:, None] <= i[None, :])
    c[:, K_ID:K_ID + P] = i[:, None] == i[None, :]
    return c


def kernel(**inputs):
    import numpy as np
    import concourse.bacc as bacc
    from concourse.bass_utils import run_bass_kernel_spmd as run

    a = {k: np.asarray(v) for k, v in inputs.items()}
    x, par, gain0 = _layouts(a)
    arrays = {"xt": x, "par": par, "gain0": gain0, "cst": _constants()}
    weights = ["ffn1_w_gate", "ffn2_w_gate", "ffn1_w_up", "ffn2_w_up", "ffn1_w_down", "ffn2_w_down", "w_in", "w_out"]
    for n in weights:
        arrays[n] = np.ascontiguousarray(a[n])
    nc = bacc.Bacc("TRN2", target_bir_lowering=False, num_devices=1)
    ap = {n: nc.dram_tensor(f"in_{n}", v.shape, F32, kind="ExternalInput").ap() for n, v in arrays.items()}
    out = nc.dram_tensor("out_x", (P, KT, SEQ), F32, kind="ExternalOutput").ap()
    w = [ap[n] for n in weights]
    trunk(nc, ap["xt"], ap["par"], ap["gain0"], ap["cst"], w[0:2], w[2:4], w[4:6], w[6], w[7], out)
    r = run(nc, [{f"in_{n}": v for n, v in arrays.items()}], core_ids=[0])
    y = np.asarray(r.results[0]["out_x"])
    return np.ascontiguousarray(y.transpose(1, 0, 2).reshape(D, SEQ).T)[None]
```
